# Optimizing a Trainium2 kernel written in Bass

```python
import math
import jax, jax.numpy as jnp
from jax import lax
import numpy as np

D_MODEL = 1024
BATCH = 1
SEQ = 512
DEPTH = 2

N_META = 16
D_ATTN = 512
D_REC = 512
D_MIX = D_ATTN + D_REC
ATTN_HEADS = 4
ATTN_HEAD_DIM = 64
V_HEAD_DIM = 2 * ATTN_HEAD_DIM
ROPE_DIM = ATTN_HEAD_DIM // 4
ROPE_THETA = 500000.0
REC_BLOCKS = 8
REC_BLOCK_DIM = D_REC // REC_BLOCKS
CONV_WIDTH = 4
LRU_C = 8.0
D_FF = -(-8 * D_MODEL // (3 * 256)) * 256
Q_BLOCK = 128
EPS = 1e-6
N_IN = 3 * D_ATTN + 2 * D_REC


def rms_norm(x, g):
    xf = x.astype(jnp.float32)
    y = xf * lax.rsqrt(jnp.mean(xf * xf, axis=-1, keepdims=True) + EPS)
    return (y * g.astype(jnp.float32)).astype(x.dtype)

def rope_tables(T):
    inv = ROPE_THETA ** (-jnp.arange(0, ROPE_DIM, 2, dtype=jnp.float32) / ROPE_DIM)
    ang = jnp.arange(T, dtype=jnp.float32)[:, None] * inv[None, :]
    return jnp.cos(ang), jnp.sin(ang)

def apply_partial_rope(x, cos, sin):
    half = ROPE_DIM // 2
    c = cos[None, :, None, None, :].astype(x.dtype)
    s = sin[None, :, None, None, :].astype(x.dtype)
    x1 = x[..., :half]
    x2 = x[..., half:ROPE_DIM]
    return jnp.concatenate([x1 * c - x2 * s, x2 * c + x1 * s, x[..., ROPE_DIM:]], axis=-1)

def diff_attention(q, k, v, lam):
    B, T, H = q.shape[:3]
    nb = -(-T // Q_BLOCK)
    Tp = nb * Q_BLOCK
    padw = ((0, 0), (0, Tp - T), (0, 0), (0, 0), (0, 0))
    q = jnp.pad(q, padw)
    k = jnp.pad(k, padw)
    v = jnp.pad(v, padw[:4])
    qb = q.reshape(B, nb, Q_BLOCK, H, 2, ATTN_HEAD_DIM).transpose(1, 0, 2, 3, 4, 5)
    starts = jnp.arange(nb) * Q_BLOCK
    kpos = jnp.arange(Tp)
    scale = ATTN_HEAD_DIM ** -0.5

    def one_block(args):
        qblk, start = args
        s = jnp.einsum('bqhcd,bkhcd->bhcqk', qblk, k,
                       preferred_element_type=jnp.float32) * scale
        qpos = start + jnp.arange(Q_BLOCK)
        s = jnp.where(qpos[:, None] >= kpos[None, :], s, -jnp.inf)
        p = jax.nn.softmax(s, axis=-1)
        a = p[:, :, 0] - lam * p[:, :, 1]
        return jnp.einsum('bhqk,bkhe->bqhe', a.astype(v.dtype), v)

    o = lax.map(one_block, (qb, starts))
    return o.transpose(1, 0, 2, 3, 4).reshape(B, Tp, H, V_HEAD_DIM)[:, :T]

def rg_lru_branch(xr, gate, conv_w, conv_b, w_rg, b_rg, w_ig, b_ig, lru_L):
    B, T, _ = xr.shape
    xc = lax.conv_general_dilated(
        xr, conv_w[:, None, :].astype(xr.dtype), window_strides=(1,),
        padding=[(CONV_WIDTH - 1, 0)], dimension_numbers=('NWC', 'WIO', 'NWC'),
        feature_group_count=D_REC) + conv_b.astype(xr.dtype)
    xb = xc.reshape(B, T, REC_BLOCKS, REC_BLOCK_DIM)
    r = jax.nn.sigmoid((jnp.einsum('btnd,nde->btne', xb, w_rg).reshape(B, T, D_REC)
                        + b_rg).astype(jnp.float32))
    i = jax.nn.sigmoid((jnp.einsum('btnd,nde->btne', xb, w_ig).reshape(B, T, D_REC)
                        + b_ig).astype(jnp.float32))
    log_a = LRU_C * r * jax.nn.log_sigmoid(lru_L.astype(jnp.float32))
    a = jnp.exp(log_a)
    mult = jnp.sqrt(jnp.maximum(-jnp.expm1(2.0 * log_a), 0.0))
    mult = jnp.where(jnp.arange(T)[None, :, None] == 0, 1.0, mult)
    u = mult * i * xc.astype(jnp.float32)

    def combine(left, right):
        a1, b1 = left
        a2, b2 = right
        return a1 * a2, a2 * b1 + b2

    _, h = lax.associative_scan(combine, (a, u), axis=1)
    y = h * jax.nn.gelu(gate.astype(jnp.float32))
    return y.astype(xr.dtype)

def first_inputs(seed: int = 0) -> dict:
    key = jax.random.key(seed)
    ks = jax.random.split(key, 24)
    f32 = jnp.float32
    L = DEPTH

    def nrm(k, shape, scale):
        return jax.random.normal(k, shape, f32) * scale

    u = jax.random.uniform(ks[15], (L, D_REC), f32, 0.9, 0.999)
    s = u ** (1.0 / LRU_C)
    lru_L = jnp.log(s) - jnp.log1p(-s)
    return {
        "x": nrm(ks[0], (BATCH, SEQ, D_MODEL), 1.0),
        "meta_tokens": nrm(ks[1], (N_META, D_MODEL), 1.0),
        "norm_mix_g": 1.0 + nrm(ks[2], (L, D_MODEL), 0.02),
        "w_in": nrm(ks[3], (L, D_MODEL, N_IN), D_MODEL ** -0.5),
        "q_norm_g": 1.0 + nrm(ks[4], (L, ATTN_HEAD_DIM), 0.02),
        "k_norm_g": 1.0 + nrm(ks[5], (L, ATTN_HEAD_DIM), 0.02),
        "lambda_q1": nrm(ks[6], (L, ATTN_HEAD_DIM), 0.1),
        "lambda_k1": nrm(ks[7], (L, ATTN_HEAD_DIM), 0.1),
        "lambda_q2": nrm(ks[8], (L, ATTN_HEAD_DIM), 0.1),
        "lambda_k2": nrm(ks[9], (L, ATTN_HEAD_DIM), 0.1),
        "subln_g": 1.0 + nrm(ks[10], (L, V_HEAD_DIM), 0.02),
        "conv_w": nrm(ks[11], (L, CONV_WIDTH, D_REC), CONV_WIDTH ** -0.5),
        "conv_b": nrm(ks[12], (L, D_REC), 0.01),
        "w_rg": nrm(ks[13], (L, REC_BLOCKS, REC_BLOCK_DIM, REC_BLOCK_DIM), REC_BLOCK_DIM ** -0.5),
        "b_rg": nrm(ks[14], (L, D_REC), 0.01),
        "w_ig": nrm(ks[16], (L, REC_BLOCKS, REC_BLOCK_DIM, REC_BLOCK_DIM), REC_BLOCK_DIM ** -0.5),
        "b_ig": nrm(ks[17], (L, D_REC), 0.01),
        "lru_L": lru_L,
        "rec_norm_g": 1.0 + nrm(ks[18], (L, D_REC), 0.02),
        "w_out": nrm(ks[19], (L, D_MIX, D_MODEL), D_MIX ** -0.5),
        "norm_ffn_g": 1.0 + nrm(ks[20], (L, D_MODEL), 0.02),
        "w_gu": nrm(ks[21], (L, D_MODEL, 2 * D_FF), D_MODEL ** -0.5),
        "w_down": nrm(ks[22], (L, D_FF, D_MODEL), D_FF ** -0.5),
    }

def first_block(x, meta_tokens, norm_mix_g, w_in, q_norm_g, k_norm_g, lambda_q1, lambda_k1,
              lambda_q2, lambda_k2, subln_g, conv_w, conv_b, w_rg, b_rg, w_ig, b_ig, lru_L,
              rec_norm_g, w_out, norm_ffn_g, w_gu, w_down):
    B = x.shape[0]
    meta = jnp.broadcast_to(meta_tokens.astype(x.dtype)[None], (B, N_META, D_MODEL))
    h = jnp.concatenate([meta, x], axis=1)
    T = h.shape[1]
    cos, sin = rope_tables(T)
    splits = [D_ATTN, 2 * D_ATTN, 3 * D_ATTN, 3 * D_ATTN + D_REC]

    for l in range(DEPTH):
        lam_init = 0.8 - 0.6 * math.exp(-0.3 * l)
        hn = rms_norm(h, norm_mix_g[l])
        proj = hn @ w_in[l]
        q, k, v, xr, gate = jnp.split(proj, splits, axis=-1)
        q = q.reshape(B, T, ATTN_HEADS, 2, ATTN_HEAD_DIM)
        k = k.reshape(B, T, ATTN_HEADS, 2, ATTN_HEAD_DIM)
        v = v.reshape(B, T, ATTN_HEADS, V_HEAD_DIM)
        q = apply_partial_rope(rms_norm(q, q_norm_g[l]), cos, sin)
        k = apply_partial_rope(rms_norm(k, k_norm_g[l]), cos, sin)
        lam = (jnp.exp(jnp.sum(lambda_q1[l].astype(jnp.float32) * lambda_k1[l].astype(jnp.float32)))
               - jnp.exp(jnp.sum(lambda_q2[l].astype(jnp.float32) * lambda_k2[l].astype(jnp.float32)))
               + lam_init)
        o_attn = diff_attention(q, k, v, lam)
        o_attn = (rms_norm(o_attn, subln_g[l]) * (1.0 - lam_init)).reshape(B, T, D_ATTN)
        o_rec = rg_lru_branch(xr, gate, conv_w[l], conv_b[l], w_rg[l], b_rg[l],
                              w_ig[l], b_ig[l], lru_L[l])
        o_rec = rms_norm(o_rec, rec_norm_g[l])
        h = h + jnp.concatenate([o_attn, o_rec], axis=-1) @ w_out[l]
        hn = rms_norm(h, norm_ffn_g[l])
        g, u = jnp.split(hn @ w_gu[l], [D_FF], axis=-1)
        h = h + (jax.nn.silu(g) * u) @ w_down[l]

    return h[:, N_META:, :]


CHUNK = 64
QBLOCK = 128
MIX_WIDTH = D_MODEL
HEAD_DIM = 64
CONV_WIDTH_2 = MIX_WIDTH // 4
CONV_K = 3
ATT_WIDTH = (MIX_WIDTH - CONV_WIDTH_2) // 2
DSA_HEADS = ATT_WIDTH // HEAD_DIM
CHK_HEADS = ATT_WIDTH // HEAD_DIM
ROPE_DIM_2 = HEAD_DIM // 4
IDX_HEADS = 8
IDX_DIM = 32
IDX_ROPE_DIM = IDX_DIM // 4
TOPK_MAX = 256
BAND_CHUNKS = 8
REL_CLIP = 128
REL_SIZE = (CHUNK - 1) + REL_CLIP + 1
MEM_LEN = 256
MEM_HEADS = 4
MEM_HEAD_DIM = D_MODEL // MEM_HEADS
D_FF_2 = 4 * D_MODEL
LN_EPS = 1e-5
ALPHA = (2.0 * DEPTH) ** 0.25
BETA = (8.0 * DEPTH) ** -0.25
IN_SIZES = (CONV_WIDTH_2, CONV_WIDTH_2, CONV_WIDTH_2,
            DSA_HEADS * HEAD_DIM, HEAD_DIM, HEAD_DIM,
            IDX_HEADS * IDX_DIM, IDX_DIM, IDX_HEADS,
            CHK_HEADS * HEAD_DIM, CHK_HEADS * HEAD_DIM, CHK_HEADS * HEAD_DIM)
IN_WIDTH = sum(IN_SIZES)


def layer_norm(x, g, b):
    xf = x.astype(jnp.float32)
    mu = jnp.mean(xf, axis=-1, keepdims=True)
    var = jnp.mean(jnp.square(xf - mu), axis=-1, keepdims=True)
    y = (xf - mu) * lax.rsqrt(var + LN_EPS) * g.astype(jnp.float32) + b.astype(jnp.float32)
    return y.astype(x.dtype)

def partial_rope(x, positions, rot_dim):
    half = rot_dim // 2
    inv_freq = jnp.power(jnp.float32(ROPE_THETA), -jnp.arange(half, dtype=jnp.float32) / half)
    ang = positions.astype(jnp.float32)[..., None] * inv_freq
    cos = jnp.cos(ang)[:, :, None, :]
    sin = jnp.sin(ang)[:, :, None, :]
    x1 = x[..., :half].astype(jnp.float32)
    x2 = x[..., half:rot_dim].astype(jnp.float32)
    rot = jnp.concatenate([x1 * cos - x2 * sin, x2 * cos + x1 * sin], axis=-1)
    return jnp.concatenate([rot.astype(x.dtype), x[..., rot_dim:]], axis=-1)

def short_conv_mixer(gate_b, gate_c, h, conv_w):
    u = gate_c * h
    S = u.shape[1]
    u_pad = jnp.pad(u, ((0, 0), (CONV_K - 1, 0), (0, 0)))
    y = conv_w[0] * u_pad[:, 0:S]
    for j in range(1, CONV_K):
        y = y + conv_w[j] * u_pad[:, j:j + S]
    return gate_b * y

def dsa_attention(q, k, v, iq, ik, iw):
    B_, S, H, Dh = q.shape
    nb = S // QBLOCK
    topk = min(TOPK_MAX, S // 4)
    scale = Dh ** -0.5
    key_chunk = jnp.arange(S) // CHUNK
    iw = iw * (IDX_HEADS ** -0.5)

    def to_blocks(a):
        return jnp.moveaxis(a.reshape((B_, nb, QBLOCK) + a.shape[2:]), 1, 0)

    def one_block(args):
        bi, qb, iqb, iwb = args
        q_chunk = (bi * QBLOCK + jnp.arange(QBLOCK)) // CHUNK
        logits = jnp.einsum('bqhd,bsd->bqhs', iqb, ik)
        score = jnp.einsum('bqh,bqhs->bqs', iwb, jax.nn.relu(logits)).astype(jnp.float32)
        admissible = key_chunk[None, :] <= q_chunk[:, None]
        score = jnp.where(admissible[None], score, -jnp.inf)
        _, idx = lax.top_k(score, topk)
        valid = (idx // CHUNK) <= q_chunk[None, :, None]
        k_sel = jax.vmap(lambda a, ii: a[ii])(k, idx)
        v_sel = jax.vmap(lambda a, ii: a[ii])(v, idx)
        s = jnp.einsum('bqhd,bqkd->bhqk', qb, k_sel).astype(jnp.float32) * scale
        s = jnp.where(valid[:, None], s, -jnp.inf)
        p = jax.nn.softmax(s, axis=-1)
        return jnp.einsum('bhqk,bqkd->bqhd', p.astype(v_sel.dtype), v_sel)

    out = lax.map(one_block, (jnp.arange(nb), to_blocks(q), to_blocks(iq), to_blocks(iw)))
    return jnp.moveaxis(out, 0, 1).reshape(B_, S, H * Dh)

def chunk_band_attention(q, k, v, rel_bias):
    B_, S, H, Dh = q.shape
    nc = S // CHUNK
    band = (BAND_CHUNKS + 1) * CHUNK
    pad = BAND_CHUNKS * CHUNK
    scale = Dh ** -0.5
    k_pad = jnp.pad(k, ((0, 0), (pad, 0), (0, 0), (0, 0)))
    v_pad = jnp.pad(v, ((0, 0), (pad, 0), (0, 0), (0, 0)))
    i = jnp.arange(CHUNK)[:, None]
    j = jnp.arange(band)[None, :]
    rel = i - j + pad
    rel_idx = jnp.clip(rel, -(CHUNK - 1), REL_CLIP) + (CHUNK - 1)
    bias = rel_bias[:, rel_idx].astype(jnp.float32)
    q_chunks = jnp.moveaxis(q.reshape(B_, nc, CHUNK, H, Dh), 1, 0)

    def one_chunk(args):
        c, qc = args
        start = c * CHUNK
        kc = lax.dynamic_slice_in_dim(k_pad, start, band, axis=1)
        vc = lax.dynamic_slice_in_dim(v_pad, start, band, axis=1)
        s = jnp.einsum('bqhd,bkhd->bhqk', qc, kc).astype(jnp.float32) * scale + bias
        valid = jnp.arange(band) >= (pad - start)
        s = jnp.where(valid, s, -jnp.inf)
        p = jax.nn.softmax(s, axis=-1)
        return jnp.einsum('bhqk,bkhd->bqhd', p.astype(vc.dtype), vc)

    out = lax.map(one_chunk, (jnp.arange(nc), q_chunks))
    return jnp.moveaxis(out, 0, 1).reshape(B_, S, H * Dh)

def hybrid_mixer(x, positions, w_in, conv_w, rel_bias, w_out):
    B_, S, _ = x.shape
    proj = jnp.einsum('bsd,dp->bsp', x, w_in)
    offs = np.cumsum(np.array(IN_SIZES))[:-1].tolist()
    (cb, cc, ch, dq, dk, dv, iq, ik, iw, cq, ck, cv) = jnp.split(proj, offs, axis=-1)
    y_conv = short_conv_mixer(cb, cc, ch, conv_w)
    dq = partial_rope(dq.reshape(B_, S, DSA_HEADS, HEAD_DIM), positions, ROPE_DIM_2)
    dk = partial_rope(dk.reshape(B_, S, 1, HEAD_DIM), positions, ROPE_DIM_2)[:, :, 0]
    iq = partial_rope(iq.reshape(B_, S, IDX_HEADS, IDX_DIM), positions, IDX_ROPE_DIM)
    ik = partial_rope(ik.reshape(B_, S, 1, IDX_DIM), positions, IDX_ROPE_DIM)[:, :, 0]
    y_dsa = dsa_attention(dq, dk, dv, iq, ik, iw)
    cq = cq.reshape(B_, S, CHK_HEADS, HEAD_DIM)
    ck = ck.reshape(B_, S, CHK_HEADS, HEAD_DIM)
    cv = cv.reshape(B_, S, CHK_HEADS, HEAD_DIM)
    y_chk = chunk_band_attention(cq, ck, cv, rel_bias)
    y = jnp.concatenate([y_conv, y_dsa, y_chk], axis=-1)
    return jnp.einsum('bsm,md->bsd', y, w_out)

def memory_cross_attention(x, mem, w_q, w_kv, w_o):
    B_, S, _ = x.shape
    M = mem.shape[1]
    q = jnp.einsum('bsd,de->bse', x, w_q).reshape(B_, S, MEM_HEADS, MEM_HEAD_DIM)
    k, v = jnp.split(jnp.einsum('bmd,de->bme', mem, w_kv), 2, axis=-1)
    k = k.reshape(B_, M, MEM_HEADS, MEM_HEAD_DIM)
    v = v.reshape(B_, M, MEM_HEADS, MEM_HEAD_DIM)
    s = jnp.einsum('bshd,bmhd->bhsm', q, k).astype(jnp.float32) * (MEM_HEAD_DIM ** -0.5)
    p = jax.nn.softmax(s, axis=-1)
    o = jnp.einsum('bhsm,bmhd->bshd', p.astype(v.dtype), v).reshape(B_, S, D_MODEL)
    return jnp.einsum('bse,ed->bsd', o, w_o)

def squared_relu_mlp(x, w1, w2):
    h = jnp.square(jax.nn.relu(jnp.einsum('bsd,df->bsf', x, w1)))
    return jnp.einsum('bsf,fd->bsd', h, w2)

def second_inputs(seed: int = 0) -> dict:
    key = jax.random.key(seed)
    ks = jax.random.split(key, 20)
    f32 = jnp.float32
    nrm = lambda k, shape, s: jax.random.normal(k, shape, f32) * s
    x = nrm(ks[0], (BATCH, SEQ, D_MODEL), 1.0)
    mem = nrm(ks[1], (BATCH, MEM_LEN, D_MODEL), 1.0)
    offset = jax.random.randint(ks[2], (BATCH,), 0, 4096, dtype=jnp.int32)
    positions = (offset[:, None] + jnp.arange(SEQ, dtype=jnp.int32)[None, :]).astype(jnp.int32)
    return {
        'x': x,
        'mem': mem,
        'positions': positions,
        'w_in': nrm(ks[3], (DEPTH, D_MODEL, IN_WIDTH), D_MODEL ** -0.5),
        'conv_w': nrm(ks[4], (DEPTH, CONV_K, CONV_WIDTH_2), CONV_K ** -0.5),
        'rel_bias': nrm(ks[5], (DEPTH, CHK_HEADS, REL_SIZE), 0.5),
        'w_mix_out': nrm(ks[6], (DEPTH, MIX_WIDTH, D_MODEL), BETA * MIX_WIDTH ** -0.5),
        'ln1_g': 1.0 + nrm(ks[7], (DEPTH, D_MODEL), 0.02),
        'ln1_b': nrm(ks[8], (DEPTH, D_MODEL), 0.02),
        'w_mq': nrm(ks[9], (DEPTH, D_MODEL, D_MODEL), D_MODEL ** -0.5),
        'w_mkv': nrm(ks[10], (DEPTH, D_MODEL, 2 * D_MODEL), D_MODEL ** -0.5),
        'w_mo': nrm(ks[11], (DEPTH, D_MODEL, D_MODEL), BETA * D_MODEL ** -0.5),
        'ln2_g': 1.0 + nrm(ks[12], (DEPTH, D_MODEL), 0.02),
        'ln2_b': nrm(ks[13], (DEPTH, D_MODEL), 0.02),
        'w_ff1': nrm(ks[14], (DEPTH, D_MODEL, D_FF_2), D_MODEL ** -0.5),
        'w_ff2': nrm(ks[15], (DEPTH, D_FF_2, D_MODEL), BETA * D_FF_2 ** -0.5),
        'ln3_g': 1.0 + nrm(ks[16], (DEPTH, D_MODEL), 0.02),
        'ln3_b': nrm(ks[17], (DEPTH, D_MODEL), 0.02),
    }

def second_block(x, mem, positions, w_in, conv_w, rel_bias, w_mix_out, ln1_g, ln1_b,
              w_mq, w_mkv, w_mo, ln2_g, ln2_b, w_ff1, w_ff2, ln3_g, ln3_b):
    for l in range(DEPTH):
        mix = hybrid_mixer(x, positions, w_in[l], conv_w[l], rel_bias[l], w_mix_out[l])
        x = layer_norm(ALPHA * x + mix, ln1_g[l], ln1_b[l])
        cross = memory_cross_attention(x, mem, w_mq[l], w_mkv[l], w_mo[l])
        x = layer_norm(ALPHA * x + cross, ln2_g[l], ln2_b[l])
        ff = squared_relu_mlp(x, w_ff1[l], w_ff2[l])
        x = layer_norm(ALPHA * x + ff, ln3_g[l], ln3_b[l])
    return x


def setup_inputs(seed=0):
    out = dict(first_inputs(seed))
    for name, value in second_inputs(seed + 1).items():
        if name != "x":
            out[name + "_2"] = value
    return out


def reference(
    x, meta_tokens, norm_mix_g, w_in, q_norm_g, k_norm_g, lambda_q1, lambda_k1, lambda_q2,
    lambda_k2, subln_g, conv_w, conv_b, w_rg, b_rg, w_ig, b_ig, lru_L, rec_norm_g, w_out,
    norm_ffn_g, w_gu, w_down, mem_2, positions_2, w_in_2, conv_w_2, rel_bias_2, w_mix_out_2,
    ln1_g_2, ln1_b_2, w_mq_2, w_mkv_2, w_mo_2, ln2_g_2, ln2_b_2, w_ff1_2, w_ff2_2, ln3_g_2,
    ln3_b_2,
):
    x = first_block(
        x, meta_tokens, norm_mix_g, w_in, q_norm_g, k_norm_g, lambda_q1, lambda_k1, lambda_q2,
        lambda_k2, subln_g, conv_w, conv_b, w_rg, b_rg, w_ig, b_ig, lru_L, rec_norm_g, w_out,
        norm_ffn_g, w_gu, w_down,
    )
    return second_block(
        x, mem_2, positions_2, w_in_2, conv_w_2, rel_bias_2, w_mix_out_2, ln1_g_2, ln1_b_2,
        w_mq_2, w_mkv_2, w_mo_2, ln2_g_2, ln2_b_2, w_ff1_2, w_ff2_2, ln3_g_2, ln3_b_2,
    )


_drawn_inputs = setup_inputs


def setup_inputs(seed=0):
    import zlib

    import numpy as np

    out = dict(_drawn_inputs(seed))
    spreads = {}
    factors = {'q_norm_g': 3.429, 'k_norm_g': 3.094, 'lambda_q2': 2.729, 'b_rg': 8.0, 'b_ig': 8.0}
    for name, (base, spread) in spreads.items():
        noise = np.random.default_rng([zlib.crc32(name.encode()), seed]).standard_normal(out[name].shape)
        drawn = base * np.exp(spread * noise) if base else spread * noise
        out[name] = __import__('jax').numpy.asarray(drawn.astype(out[name].dtype))
    for name, factor in factors.items():
        out[name] = (out[name] * factor).astype(out[name].dtype)
    return out
```

```python
import math
from contextlib import ExitStack

import numpy as np

import concourse.bass as bass
from concourse import mybir

F32 = mybir.dt.float32
F32R = mybir.dt.float32r
BF16 = mybir.dt.bfloat16
I32 = mybir.dt.int32
ALU = mybir.AluOpType
ACT = mybir.ActivationFunctionType
AX = mybir.AxisListType

P = 128
D = 1024
DC = D // P
DEPTH = 2
SEQ = 512
META = 16
T1 = SEQ + META
T2 = SEQ
BANK = 512

HEADS = 4
HEAD_DIM = 64
ROPE_THETA = 500000.0
REC_TILES = 4
LRU_C = 8.0
D_FF = 2816
FF_TILES = D_FF // P
EPS = 1e-6
FF_GROUPS = [(0, 8), (8, 15), (15, 22)]

FF2_TILES = 4 * D // P
FF2_GROUPS = [(g, g + 8) for g in range(0, FF2_TILES, 8)]
CONV_TILES = 2
DSA_PAIRS = 3
CHK_PAIRS = 3
IDX_HEADS = 8
IDX_DIM = 32
CHUNK = 64
TOPK = min(256, SEQ // 4)
MEM = 256
MEM_HEADS = 4
MEM_DIM = D // MEM_HEADS
LN_EPS = 1e-5
ALPHA = (2.0 * DEPTH) ** 0.25
REL_CLIP = 128
TOK_V_CHK, TOK_V_DSA, TOK_IW = 0, 384, 448
TOK_COLS = 456

STAGING, PARTS, TEMPS = 3, 3, 9
UNITS = 3
LATENCY, POLL = 0.1, 0.1

MASKED = float(2.0 ** 100)
TAKEN = -float(2.0 ** 127)
INADMISSIBLE = -float(2.0 ** 126)

C_IDENT, C_BLOCK, C_ROT16, C_ROT8, C_INV = 0, 128, 256, 384, 512
C_CAUSAL, C_CHUNK = 514, 642
C_COS1, C_SIN1 = 770, 770 + T1
C_COLS = 770 + 2 * T1

PARAMS1 = [("mix_g", DC), ("q_g", 1), ("k_g", 1), ("subln_g", 1), ("conv_w", 16), ("conv_b", 4),
           ("b_rg", 4), ("b_ig", 4), ("lru", 4), ("rec_g", 4), ("ffn_g", DC)]
PARAMS2 = [("conv_w2", 6), ("ln1_g", DC), ("ln1_b", DC), ("ln2_g", DC), ("ln2_b", DC),
           ("ln3_g", DC), ("ln3_b", DC)]


def columns(params):
    at, where = 0, {}
    for name, n in params:
        where[name] = (at, n)
        at += n
    return where, at


WHERE1, NP1 = columns(PARAMS1)
WHERE2, NP2 = columns(PARAMS2)

TILES2 = ([("iq", n) for n in range(2)] + [("ik", 0)]
          + [("cb", n) for n in range(2)] + [("cc", n) for n in range(2)] + [("ch", n) for n in range(2)]
          + [("cq", n) for n in range(3)] + [("ck", n) for n in range(3)]
          + [("dk", 0)] + [("dq", n) for n in range(3)])
SLOT2 = {tile: n for n, tile in enumerate(TILES2)}


class Instruction:

    @staticmethod
    def columns(out):
        return math.prod(out.shape[1:])

    def matmul(self, out, weights, moving, **k):
        n = self.columns(out)
        passes = 4 if moving.dtype == F32 or (moving.dtype == F32R and n < 256) else 1
        return (lambda e: e.matmul(out, weights, moving, **k)), passes * n

    def transpose(self, out, src, ident):
        return (lambda e: e.transpose(out, src, ident)), 2 * self.columns(out)

    def activation(self, out, *a, **k):
        return (lambda e: e.activation(out, *a, **k)), self.columns(out)

    def tensor_tensor(self, out, *a, **k):
        return (lambda e: e.tensor_tensor(out, *a, **k)), self.columns(out)

    def scalar_tensor_tensor(self, out, *a, **k):
        return (lambda e: e.scalar_tensor_tensor(out, *a, **k)), self.columns(out)

    def tensor_scalar(self, out, *a, **k):
        return (lambda e: e.tensor_scalar(out, *a, **k)), self.columns(out) // 2

    def tensor_copy(self, out, src):
        return (lambda e: e.tensor_copy(out, src)), self.columns(out)

    def memset(self, out, value):
        return (lambda e: e.memset(out, value)), self.columns(out) // 2

    def reduce_max(self, out, src, axis):
        return (lambda e: e.reduce_max(out, src, axis)), self.columns(src)

    def reduce_sum(self, out, src, axis):
        return (lambda e: e.reduce_sum(out, src, axis)), self.columns(src)

    def reciprocal(self, out, src):
        return (lambda e: e.reciprocal(out, src)), 6 * self.columns(out)

    def tensor_tensor_scan(self, out, *a, **k):
        return (lambda e: e.tensor_tensor_scan(out, *a, **k)), 2 * self.columns(out)

    def max(self, out, src):
        return (lambda e: e.max(out, src)), self.columns(src)

    def match_replace(self, out, *a):
        return (lambda e: e.match_replace(out, *a)), self.columns(out)


INSTRUCTION = Instruction()


class Engine:

    queued, all = 0, []
    reached = {}
    latest = 0.0

    def __init__(self, sem, fixed=0.0, per_column=0.0):
        self.sem, self.count, self.steps, self.seen = sem, 0, [], {}
        self.fixed, self.per_column, self.clock = fixed, per_column, 0.0

    def wait(self, *marks):
        for mark in marks:
            if mark is None:
                continue
            if isinstance(mark, list):
                self.wait(*mark)
                continue
            sem, value = mark
            self.clock = max(self.clock, Engine.reached.get((id(sem), value), 0.0))
            if self.seen.get(id(sem), 0) < value:
                self.seen[id(sem)] = value
                self.steps.append(lambda e, sem=sem, value=value: e.wait_ge(sem, value))

    def do(self, step, *after, signal=True):
        self.wait(*after)
        Engine.queued += 1
        issue, columns = step(INSTRUCTION)
        self.clock += self.fixed + self.per_column * columns
        Engine.latest = max(Engine.latest, self.clock + LATENCY)
        if not signal:
            self.steps.append(issue)
            return None
        self.count += 1
        self.steps.append(lambda e: issue(e).then_inc(self.sem, 1))
        Engine.reached[(id(self.sem), self.count)] = self.clock + LATENCY
        return (self.sem, self.count)

    def dma(self, out, src, landed, *after):
        self.wait(*after)
        landed.count += 16
        self.steps.append(lambda e: e.dma_start(out, src).then_inc(landed.sem, 16))
        return (landed.sem, landed.count)


class Landing:

    def __init__(self, sem):
        self.sem, self.count = sem, 0


class Buffer:

    def __init__(self, ap):
        self.ap, self.readers = ap, []

    def release(self, *readers):
        assert self.readers is None
        self.readers = list(readers)


class Pool:

    def __init__(self, aps):
        self.free = [Buffer(ap) for ap in aps]

    def get(self):
        while not self.free:
            yield
        return self.take()

    def get_all(self, n):
        while len(self.free) < n:
            yield
        return [self.take() for _ in range(n)]

    def take(self):
        buf = self.free.pop(0)
        buf.before, buf.readers = buf.readers, None
        return buf

    def give(self, buf, *readers):
        buf.release(*readers)
        self.free.append(buf)


def spans(width):
    if width <= BANK:
        return [(0, width, 0)]
    half = width // 2
    return [(0, half, 0), (half, width, BANK)]


def across(slot, width):
    if width <= BANK:
        return slot[:, 0:width]
    return slot[:, :].rearrange("p (b n) -> p b n", b=2)[:, :, 0:width // 2]


def along(row, width):
    if width <= BANK:
        return row
    return row.rearrange("p (b n) -> p b n", b=2)


def together(*generators):
    now = Engine.all[0].clock
    order, active, idle = 0, [], 0
    for g in generators:
        active.append((now, order, g))
        order += 1
    while active:
        now, turn, g = first = min(active, key=lambda entry: entry[:2])
        active.remove(first)
        before, Engine.latest = Engine.queued, now
        more = next(g, g)
        idle = 0 if Engine.queued > before else idle + 1
        if idle > 10000:
            raise AssertionError("no generator can go on")
        then = Engine.latest if Engine.queued > before else now + POLL
        if more is g:
            continue
        active.append((then, turn, g))
        if more is not None:
            active.append((then, order, more))
            order += 1


def several(generators, at_once):
    running = [0]

    def counted(g):
        yield from g
        running[0] -= 1
    for g in generators:
        while running[0] >= at_once:
            yield
        running[0] += 1
        yield counted(g)
    while running[0]:
        yield


def build(nc, t, out):
    with ExitStack() as ctx:
        def sb(name, cols, dt=F32):
            return ctx.enter_context(nc.sbuf_tensor(name, [P] + list(cols), dt))

        def sem(name):
            return ctx.enter_context(nc.semaphore(name))

        mem = dict(
            x=sb("x_residual", [DC, T1]),
            act=sb("act_hi_lo", [2, DC * T1 + P - META], F32R),
            hid=sb("hidden_hi_lo", [2, DC * T1], F32R),
            arena=sb("arena", [12576]),
            consts=sb("consts", [C_CAUSAL]),
            rope=sb("rope_tables", [4, T1]),
            ones=sb("ones", [P]),
            ident_big=sb("ident_big", [P], BF16),
            causal=sb("causal_mask", [P], BF16),
            select=sb("select_masks", [4, T2], BF16),
            bias=[sb(f"rel_bias{n}", [256]) for n in range(2)],
            par1=sb("params1", [DEPTH, NP1]),
            par2=sb("params2", [DEPTH, NP2]),
            lam=sb("lambdas", [DEPTH, 8]),
            lsig=sb("log_sigmoid", [DEPTH, 4]),
            small=[sb(f"small{n}", [8]) for n in range(8)],
            iw=sb("index_weights", [4, IDX_HEADS]),
            temps=[sb(f"temp{n}", [T1]) for n in range(TEMPS)],
            staging=[sb(f"weights_float32_{n}", [DC * P]) for n in range(STAGING)],
            parts=[sb(f"weights_hi_lo_{n}", [2, DC * P], F32R) for n in range(PARTS)],
            psum=[ctx.enter_context(nc.psum_tensor(f"psum{n}", [P, 2 * BANK], F32)) for n in range(4)],
        )
        names = dict(pe=sem("pe_done"), act=sem("act_done"), dve=sem("dve_done"), pool=sem("pool_done"))
        landings = {name: sem(name) for name in
                    ["landed_x0", "landed_x1", "landed_once", "landed_consts", "landed_params", "landed_gates",
                     "landed_positions", "landed_bias0", "landed_bias1", "stored_out"]
                    + [f"landed_mem{n}" for n in range(DC // 2)] + [f"landed_weights{n}" for n in range(STAGING)]}

        order = []
        Program(mem, names, landings, t, out, None, order).write()
        program = Program(mem, names, landings, t, out, order, [])
        program.write()

        block = ctx.enter_context(nc.Block())

        @block.sync
        def _(e):
            for step in program.sp.steps:
                step(e)

        @block.scalar
        def _(e):
            for step in program.act.steps:
                step(e)

        @block.vector
        def _(e):
            for step in program.dve.steps:
                step(e)

        @block.gpsimd
        def _(e):
            for step in program.pool.steps:
                step(e)

        @block.tensor
        def _(e):
            for step in program.pe.steps:
                step(e)


class Program:
    def __init__(self, mem, sems, landings, t, out, order, record):
        self.m, self.t, self.out = mem, t, out
        self.pe, self.act = Engine(sems["pe"], 0.0, 0.00042), Engine(sems["act"], 0.2, 0.00083)
        self.dve, self.pool = Engine(sems["dve"], 0.15, 0.00105), Engine(sems["pool"], 0.2, 0.0022)
        self.sp = Engine(None)
        Engine.all, Engine.reached = [self.pe, self.act, self.dve, self.pool], {}
        self.landing = {name: Landing(s) for name, s in landings.items()}
        self.order, self.record = order, record
        self.psum = Pool(mem["psum"])
        self.temps = Pool(mem["temps"])
        self.small = Pool(mem["small"])
        self.biases = Pool([(ap, f"landed_bias{n}") for n, ap in enumerate(mem["bias"])])
        self.consts = mem["consts"]
        self.ident = self.consts[:, C_IDENT:C_IDENT + P]
        self.loaded = self.split = self.used = 0
        self.parts_ready, self.staging_free, self.parts_free = {}, [[]] * STAGING, [[]] * PARTS
        self.staged_at = {}


    def piece(self, key):
        name, *at = key
        ap = self.t[name]
        if name in ("w_down", "w_ff2"):
            l, m, k0, k1 = at
            return ap[l, m, :, k0 * P:k1 * P]
        return ap[tuple(at)]

    def load_next(self):
        n = self.loaded
        if self.order is None or n >= len(self.order):
            return
        src = self.piece(self.order[n])
        slot = n % STAGING
        self.staged_at[n] = self.sp.dma(self.m["staging"][slot][:, 0:src.shape[-1]], src,
                                        self.landing[f"landed_weights{slot}"], self.staging_free[slot])
        self.loaded += 1

    def split_next(self):
        n = self.split
        self.split += 1
        if self.order is None or n >= len(self.order):
            return
        cols = self.piece(self.order[n]).shape[-1]
        src = self.m["staging"][n % STAGING][:, 0:cols]
        parts = self.m["parts"][n % PARTS]
        hi = self.act.do(lambda e: e.activation(parts[:, 0, 0:cols], src, ACT.Copy),
                         self.staged_at[n], self.parts_free[n % PARTS])
        lo = self.dve.do(lambda e: e.tensor_tensor(parts[:, 1, 0:cols], src,
                                                   parts[:, 0, 0:cols].bitcast(F32), ALU.subtract),
                         self.staged_at[n], hi)
        self.parts_ready[n] = (hi, lo)
        self.staging_free[n % STAGING] = [hi, lo]
        self.load_next()

    def weights(self, key):
        n = self.used
        self.used += 1
        self.record.append(key)
        assert self.order is None or self.order[n] == key, (self.order[n], key)
        while self.split <= n:
            if self.parts_free[self.split % PARTS] is None:
                yield
            else:
                self.split_next()
        self.parts_free[n % PARTS] = None
        while self.split < n + PARTS and self.parts_free[self.split % PARTS] is not None:
            self.split_next()
        parts = self.m["parts"][n % PARTS]
        return n, parts[:, 0, :], parts[:, 1, :], self.parts_ready.get(n, (None, None))

    def weights_used(self, n, mark):
        self.parts_free[n % PARTS] = [mark]


    def dense(self, key, chunks, width, ready):
        (result,) = yield from self.dense_together([key], chunks, width, ready)
        return result

    def dense_together(self, keys, chunks, width, ready):
        slots = yield from self.psum.get_all(len(keys))
        pieces = []
        for key in keys:
            pieces.append((yield from self.weights(key)))
        pe = self.pe
        pe.wait(*(slot.before for slot in slots))
        last = len(chunks) - 1
        marks = [None] * len(keys)
        for k, (x_hi, x_lo) in enumerate(chunks):
            hi_ready, lo_ready = ready[k] if len(ready[k]) == 2 else (ready[k], None)
            for which, (_, w_hi, w_lo, (w_hi_there, w_lo_there)) in enumerate(pieces):
                hi_k, lo_k = w_hi[:, k * P:(k + 1) * P], w_lo[:, k * P:(k + 1) * P]
                slot = slots[which].ap
                passes = ((hi_k, x_hi, w_hi_there, hi_ready), (lo_k, x_hi, w_lo_there, None),
                          (hi_k, x_lo, lo_ready, None))
                for n, (w, x, *there) in enumerate(passes):
                    pe.wait(*there)
                    for c0, c1, place in spans(width):
                        end = k == last and n == 2
                        mark = pe.do(lambda e:
                                     e.matmul(slot[:, place:place + c1 - c0], w, x[:, c0:c1],
                                              start=k == 0 and n == 0, stop=end), signal=end and c1 == width)
                marks[which] = mark
            if k < last:
                yield
        for (piece, *_), mark in zip(pieces, marks):
            self.weights_used(piece, mark)
        yield
        return list(zip(slots, marks))

    def sums(self, weights, tiles, width, ready):
        slot = yield from self.psum.get()
        self.pe.wait(slot.before)
        for k, tile in enumerate(tiles):
            self.pe.wait(ready[k])
            for c0, c1, place in spans(width):
                mark = self.pe.do(lambda e:
                                  e.matmul(slot.ap[:, place:place + c1 - c0], weights, tile[:, c0:c1],
                                           start=k == 0, stop=k == len(tiles) - 1))
        yield
        return slot, mark


    def square(self, src, width, *after):
        sq = yield from self.temps.get()
        mark = self.act.do(lambda e: e.activation(sq.ap[:, 0:width], src, ACT.Square), sq.before, *after)
        yield
        return sq, mark

    def rsqrt_mean(self, slot, width, count, eps, there):
        act, dve = self.act, self.dve
        var, root, step = yield from self.temps.get_all(3)
        v, r, s = var.ap[:, 0:width], root.ap[:, 0:width], step.ap[:, 0:width]
        there = dve.do(lambda e: e.tensor_scalar(along(v, width), across(slot.ap, width), 1.0 / count, eps,
                                                 ALU.mult, ALU.add), there, var.before)
        self.psum.give(slot, there)
        yield
        there = act.do(lambda e: e.activation(r, v, ACT.Abs_reciprocal_sqrt), there, root.before)
        there = act.do(lambda e: e.activation(s, r, ACT.Square), there, step.before)
        yield
        there = dve.do(lambda e: e.scalar_tensor_tensor(s, s, -0.5, v, ALU.mult, ALU.mult), there)
        self.temps.give(var, there)
        yield
        there = dve.do(lambda e: e.scalar_tensor_tensor(r, s, 1.5, r, ALU.add, ALU.mult), there)
        self.temps.give(step, there)
        yield
        return root, there

    def split_into(self, hi, lo, src, *after):
        a = self.act.do(lambda e: e.activation(hi, src, ACT.Copy), *after)
        b = self.dve.do(lambda e: e.tensor_tensor(lo, src, hi.bitcast(F32), ALU.subtract), a, *after)
        return [a, b]

    def split_slowly(self, n, hi, lo, src, *after):
        a = self.act.do(lambda e: e.activation(hi, src, ACT.Copy), *after)
        yield
        engine = self.pool if n % 2 else self.dve
        b = engine.do(lambda e: e.tensor_tensor(lo, src, hi.bitcast(F32), ALU.subtract), a, *after)
        return [a, b]

    def act_chunk(self, k, width):
        base = k * width
        return (self.m["act"][:, 0, base:base + width], self.m["act"][:, 1, base:base + width])

    def hid_chunk(self, k, width):
        base = k * width
        return (self.m["hid"][:, 0, base:base + width], self.m["hid"][:, 1, base:base + width])

    def par(self, l, name, k=0):
        where, tile = (WHERE1, self.m["par1"]) if name in WHERE1 else (WHERE2, self.m["par2"])
        at = where[name][0] + k
        return tile[:, l, at:at + 1]


    def start(self):
        m, t, dve = self.m, self.t, self.dve
        x = m["x"]
        self.x_landed = []
        if self.order is not None:
            for half in range(2):
                of = slice(half * DC // 2, (half + 1) * DC // 2)
                landing = self.landing[f"landed_x{half}"]
                self.sp.dma(x[:, of, 0:META], t["meta_t"][:, of], landing)
                self.x_landed.append(self.sp.dma(x[:, of, META:T1], t["x_t"][:, of], landing))
            for _ in range(STAGING):
                self.load_next()
        else:
            self.x_landed = [None, None]
        self.act.dma(m["par1"][:, :, :], t["params1"], self.landing["landed_params"])
        self.params_there = self.act.dma(m["par2"][:, :, :], t["params2"], self.landing["landed_params"])
        self.act.dma(m["rope"][:, 0:2, :], t["consts"][:, C_COS1:C_COLS].rearrange("p (a n) -> p a n", a=2),
                     self.landing["landed_consts"])
        consts = self.consts_there = self.act.dma(m["consts"][:, :], t["consts"][:, 0:C_CAUSAL],
                                                  self.landing["landed_consts"])
        once, lams = self.temps.take(), self.temps.take()
        self.act.dma(once.ap[:, 0:2 * P], t["consts"][:, C_CAUSAL:C_COS1], self.landing["landed_once"])
        once_there = self.act.dma(lams.ap[:, 0:DEPTH * 4 * HEAD_DIM], t["lambdas"], self.landing["landed_once"])
        self.ones_there = self.pool.do(lambda e: e.memset(m["ones"][:, :], 1.0))
        pad = m["act"][:, :, DC * T1:]
        self.pad_there = self.pool.do(lambda e: e.memset(pad.bitcast(F32), 0.0))
        pool = self.pool
        pool.do(lambda e: e.tensor_scalar(m["ident_big"][:, :], self.ident, MASKED, None, ALU.mult), consts)
        pool.do(lambda e: e.tensor_copy(m["causal"][:, :], once.ap[:, 0:P]), once_there)
        self.masks_there = pool.do(lambda e: e.tensor_copy(m["select"][:, 0, 0:P], once.ap[:, P:2 * P]))
        self.temps.give(once, self.masks_there)
        self.lams, self.once_there = lams, once_there
        self.lam_there, self.lsig_there = [None] * DEPTH, [None] * DEPTH

    def lambdas(self, l):
        lam, dve = self.m["lam"], self.dve
        at = 4 * HEAD_DIM * l
        init = 0.8 - 0.6 * math.exp(-0.3 * l)
        prod = yield from self.temps.get()
        row = self.lams.ap[:, at:at + 4 * HEAD_DIM].rearrange("p (c two d) -> p c two d", c=2, two=2)
        pr = prod.ap[:, 0:2 * HEAD_DIM].rearrange("p (c d) -> p c d", c=2)
        there = dve.do(lambda e: e.tensor_tensor(pr, row[:, :, 0, :], row[:, :, 1, :], ALU.mult),
                       self.once_there, self.params_there, prod.before)
        yield
        there = dve.do(lambda e: e.reduce_sum(lam[:, l, 0:2], pr, AX.X), there)
        self.temps.give(prod, there)
        yield
        there = self.act.do(lambda e: e.activation(lam[:, l, 2:4], lam[:, l, 0:2], ACT.Exp), there)
        yield
        there = dve.do(lambda e: e.tensor_tensor(lam[:, l, 4:5], lam[:, l, 3:4], lam[:, l, 2:3], ALU.subtract), there)
        yield
        there = dve.do(lambda e: e.tensor_scalar(lam[:, l, 5:6], lam[:, l, 4:5], -init, None, ALU.add), there)
        yield
        self.lam_there[l] = dve.do(lambda e: e.tensor_scalar(lam[:, l, 6:7], self.par(l, "subln_g"), 1.0 - init, None,
                                                             ALU.mult), there)
        if l == DEPTH - 1:
            self.temps.give(self.lams, self.lam_there[l])

    def log_sigmoid(self, l):
        L = self.m["par1"][:, l, WHERE1["lru"][0]:WHERE1["lru"][0] + 4]
        dve, bufs = self.dve, []
        for _ in range(2):
            bufs.append((yield from self.small.get()))
        a, y, s, acc = (b.ap[:, at:at + 4] for b in bufs for at in (0, 4))
        before = [b.before for b in bufs]
        there = dve.do(lambda e: e.tensor_scalar(a, L, -1.0, None, ALU.mult), self.params_there, *before)
        yield
        there = dve.do(lambda e: e.tensor_tensor(a, a, L, ALU.min), there)
        yield
        there = self.act.do(lambda e: e.activation(y, a, ACT.Exp), there)
        yield
        there = dve.do(lambda e: e.tensor_scalar(a, y, 2.0, None, ALU.add), there)
        yield
        there = dve.do(lambda e: e.reciprocal(a, a), there)
        yield
        there = dve.do(lambda e: e.tensor_tensor(s, y, a, ALU.mult), there)
        yield
        there = dve.do(lambda e: e.tensor_tensor(y, s, s, ALU.mult), there)
        yield
        terms = [1.0 / n for n in range(17, 0, -2)]
        there = dve.do(lambda e: e.tensor_scalar(acc, y, terms[0], terms[1], ALU.mult, ALU.add), there)
        for c in terms[2:]:
            yield
            there = dve.do(lambda e: e.tensor_tensor(acc, acc, y, ALU.mult), there)
            yield
            there = dve.do(lambda e: e.tensor_scalar(acc, acc, c, None, ALU.add), there)
        yield
        there = dve.do(lambda e: e.tensor_tensor(acc, acc, s, ALU.mult), there)
        there = dve.do(lambda e: e.tensor_scalar(a, L, 0.0, None, ALU.min), there)
        yield
        there = dve.do(lambda e: e.scalar_tensor_tensor(a, acc, -2.0, a, ALU.mult, ALU.add), there)
        yield
        there = dve.do(lambda e: e.tensor_scalar(self.m["lsig"][:, l, :], a, -LRU_C / 2, None, ALU.mult), there)
        self.lsig_there[l] = there
        for b in bufs:
            self.small.give(b, there)


    def next_input(self, k, gain, width, there, *act_free):
        x = self.m["x"][:, k, T1 - width:T1]
        hi, lo = self.act_chunk(k, width)
        if gain is None:
            return self.split_into(hi, lo, x, there, *act_free)
        a = self.act.do(lambda e: e.activation(hi, x, ACT.Copy, scale=gain), there, self.params_there, *act_free)
        b = self.dve.do(lambda e: e.scalar_tensor_tensor(lo, x, gain, hi.bitcast(F32), ALU.mult, ALU.subtract), a)
        return [a, b]

    def add_square(self, k, there):
        sq, there = yield from self.square(self.m["x"][:, k, :], T1, there)
        if k == 0:
            self.square_sum = (sq, there)
        elif k < DC - 1:
            total, before = self.square_sum
            there = self.pool.do(lambda e: e.tensor_tensor(total.ap[:, :], total.ap[:, :], sq.ap[:, :], ALU.add),
                                 before, there)
            self.temps.give(sq, there)
            self.square_sum = (total, there)
        else:
            self.last_square = (sq, there)

    def norm_root(self):
        if self.root is None:
            self.root = ()
            (a, a_there), (b, b_there) = self.square_sum, self.last_square
            stat, mark = yield from self.sums(self.m["ones"][:, :], [a.ap, b.ap], T1,
                                              [[a_there, self.ones_there], b_there])
            self.temps.give(a, mark)
            self.temps.give(b, mark)
            self.root = yield from self.rsqrt_mean(stat, T1, D, EPS, mark)
        while not self.root:
            yield
        return self.root

    def give_root(self, *readers):
        self.temps.give(self.root[0], *readers)
        self.root = None

    def normed_product(self, name, l, chunks, ready, alpha, ks, g, b, chunk, free, out):
        x, act, dve, pool, pe = self.m["x"][:, :, META:T1], self.act, self.dve, self.pool, self.pe
        half = DC // 2
        state = dict(shift=None, sums=None)
        d_there, ones = [None] * DC, self.m["ones"][:, :]
        total = yield from self.temps.get()
        added = [None] * DC

        def first(n, slot, mark):
            added[n] = dve.do(lambda e: e.scalar_tensor_tensor(x[:, n, :], x[:, n, :], alpha, slot.ap[:, 0:T2], ALU.mult,
                                                               ALU.add), mark, self.x_marks[n])
            self.psum.give(slot, added[n])
            yield
            if n == 0:
                state["total"] = added[0]
                return
            while "total" not in state or state.get("next", 1) != n:
                yield
            before = x[:, 0, :] if n == 1 else total.ap[:, 0:T2]
            state["total"] = pool.do(lambda e: e.tensor_tensor(total.ap[:, 0:T2], before, x[:, n, :], ALU.add),
                                     state["total"], added[n], total.before)
            state["next"] = n + 1

        def shift():
            while state.get("next") != half:
                yield
            slot, mark = yield from self.sums(ones, [total.ap], T2, [state["total"]])
            state["shift"] = act.do(lambda e: e.activation(total.ap[:, 0:T2], slot.ap[:, 0:T2], ACT.Copy,
                                                           scale=-1.0 / (half * P)), mark)
            self.psum.give(slot, state["shift"])
            yield
            for n in range(half, DC):
                added[n] = dve.do(lambda e: e.scalar_tensor_tensor(x[:, n, :], x[:, n, :], alpha, total.ap[:, 0:T2],
                                                                   ALU.mult, ALU.add), state["shift"], self.x_marks[n])
                yield

        def shifted(n, slot, mark):
            if n < half:
                yield from first(n, slot, mark)
                while state["shift"] is None:
                    yield
                d_there[n] = dve.do(lambda e: e.tensor_tensor(x[:, n, :], x[:, n, :], total.ap[:, 0:T2], ALU.add),
                                    state["shift"], added[n])
            else:
                while added[n] is None:
                    yield
                d_there[n] = dve.do(lambda e: e.tensor_tensor(x[:, n, :], x[:, n, :], slot.ap[:, 0:T2], ALU.add),
                                    mark, added[n])
                self.psum.give(slot, d_there[n])
            yield
            sq, there = yield from self.square(x[:, n, :], T2, d_there[n])
            if n == DC - 1:
                state["last"] = (sq, there)
                return
            while n > 0 and (state["sums"] is None or state["sums"][0] != n):
                yield
            if n == 0:
                there = pool.do(lambda e: e.tensor_scalar(sq.ap[:, 0:T2], sq.ap[:, 0:T2], LN_EPS * D / P, None, ALU.add),
                                there)
                state["sums"] = (1, sq, there, d_there[0])
                return
            _, squares, s_there, _ = state["sums"]
            plain = x[:, 0, :] if n == 1 else total2.ap[:, 0:T2]
            d_sum = pool.do(lambda e: e.tensor_tensor(total2.ap[:, 0:T2], plain, x[:, n, :], ALU.add),
                            state["sums"][3], d_there[n], total2.before)
            there = pool.do(lambda e: e.tensor_tensor(squares.ap[:, 0:T2], squares.ap[:, 0:T2], sq.ap[:, 0:T2], ALU.add),
                            there, s_there)
            self.temps.give(sq, there)
            state["sums"] = (n + 1, squares, there, d_sum)

        total2 = yield from self.temps.get()

        def products():
            for n0 in range(0, DC, 2):
                names = [(name, l, n) if ks is None else (name, l, n, *ks) for n in (n0, n0 + 1)]
                results = [] if n0 else (yield from self.dense_together(names, chunks, T2, ready))
                for n, key in zip((n0, n0 + 1), names):
                    slot, mark = results[n - n0] if results else (yield from self.dense(key, chunks, T2, ready))
                    yield shifted(n, slot, mark)
            if name == "w_mo":
                self.act_free = [mark]
            else:
                self.hid_free = [mark]

        def statistics():
            while state["sums"] is None or state["sums"][0] != DC - 1 or "last" not in state:
                yield
            _, squares, s_there, d_there7 = state["sums"]
            last_sq, last_there = state["last"]
            slot = yield from self.psum.get()
            pe.wait(slot.before)
            for at, tiles in ((0, ((total2.ap, d_there7), (x[:, DC - 1, :], d_there[DC - 1]))),
                              (BANK, ((squares.ap, s_there), (last_sq.ap, last_there)))):
                for k, (tile, there) in enumerate(tiles):
                    mark = pe.do(lambda e: e.matmul(slot.ap[:, at:at + T2], ones, tile[:, 0:T2], start=k == 0,
                                                    stop=k == 1), there)
                if at == 0:
                    mean_mark = mark
            self.temps.give(squares, mark)
            self.temps.give(last_sq, mark)
            yield
            mean, square = total2.ap[:, 0:T2], total.ap[:, 0:T2]
            m_there = act.do(lambda e: e.activation(mean, slot.ap[:, 0:T2], ACT.Copy, scale=1.0 / D), mean_mark)
            sq_there = act.do(lambda e: e.activation(square, mean, ACT.Square), m_there, d_there[:half])
            yield
            v_there = dve.do(lambda e: e.scalar_tensor_tensor(square, slot.ap[:, BANK:BANK + T2], 1.0 / D, square,
                                                              ALU.mult, ALU.subtract), sq_there, mark)
            self.psum.give(slot, m_there, v_there)
            yield
            root, step = yield from self.temps.get_all(2)
            q, st = root.ap[:, 0:T2], step.ap[:, 0:T2]
            there = act.do(lambda e: e.activation(q, square, ACT.Abs_reciprocal_sqrt), v_there, root.before)
            there = act.do(lambda e: e.activation(st, q, ACT.Square), there, step.before)
            centred = [None] * DC
            for n in (0, 2, 3):
                centred[n] = dve.do(lambda e: e.tensor_tensor(x[:, n, :], x[:, n, :], mean, ALU.subtract), m_there,
                                    d_there[n])
            for n in (1, 4, 5, 7):
                centred[n] = pool.do(lambda e: e.tensor_tensor(x[:, n, :], x[:, n, :], mean, ALU.subtract), m_there,
                                     d_there[n])
            yield
            there = dve.do(lambda e: e.scalar_tensor_tensor(st, st, -0.5, square, ALU.mult, ALU.mult), there)
            there = dve.do(lambda e: e.scalar_tensor_tensor(q, st, 1.5, q, ALU.add, ALU.mult), there)
            self.temps.give(step, there)
            self.temps.give(total, there)
            yield
            for k in range(DC):
                tmp = yield from self.temps.get()
                if k == 6:
                    centred[6] = dve.do(lambda e: e.tensor_tensor(x[:, 6, :], x[:, 6, :], mean, ALU.subtract), m_there)
                done = dve.do(lambda e: e.tensor_tensor(tmp.ap[:, 0:T2], x[:, k, :], q, ALU.mult), there, centred[k],
                              tmp.before)
                yield finished(k, tmp, done)
            self.temps.give(root, done)
            self.temps.give(total2, *centred)

        def finished(k, tmp, done):
            if chunk is None:
                out[k] = act.do(lambda e: e.activation(x[:, k, :], tmp.ap[:, 0:T2], ACT.Identity, bias=b(k), scale=g(k)),
                                done)
                self.temps.give(tmp, out[k])
                self.x_marks[k] = [out[k]]
                return
            hi, lo = chunk(k, T2)
            a = act.do(lambda e: e.activation(hi, tmp.ap[:, 0:T2], ACT.Identity, bias=b(k), scale=g(k)), done, free())
            new = act.do(lambda e: e.activation(x[:, k, :], tmp.ap[:, 0:T2], ACT.Identity, bias=b(k), scale=g(k)), done)
            self.temps.give(tmp, a, new)
            self.x_marks[k] = [new]
            yield
            engine = pool if k % 2 else dve
            c = engine.do(lambda e: e.tensor_tensor(lo, x[:, k, :], hi.bitcast(F32), ALU.subtract), a, new)
            out[k] = [a, c]

        yield shift()
        yield statistics()
        yield from products()


    def values_token_major(self, name, l, chunks, ready, tokens, cols):
        n_tiles = -(-tokens // P)
        slots = yield from self.psum.get_all(-(-n_tiles // 2))
        pe = self.pe
        for s in slots:
            pe.wait(s.before)
        pairs = len(chunks) // 2
        for piece in range(pairs):
            number, w_hi, w_lo, there = yield from self.weights((name, *l, piece))
            pe.wait(*there)
            for i in range(n_tiles):
                bank = slots[i // 2].ap[:, (i % 2) * BANK:(i % 2) * BANK + cols]
                for kk in range(2):
                    k = 2 * piece + kk
                    pe.wait(ready[k])
                    base_hi, base_lo = chunks[k]
                    for n, (xs, w) in enumerate(((base_hi, w_hi), (base_hi, w_lo), (base_lo, w_hi))):
                        mark = pe.do(lambda e:
                                     e.matmul(bank, xs(i), w[:, kk * cols:(kk + 1) * cols],
                                              start=(k == 0 and n == 0), stop=(k == len(chunks) - 1 and n == 2)),
                                     signal=(kk == 1 and n == 2))
                yield
            self.weights_used(number, mark)
        return slots, mark

    def token_chunks(self, tensor, width, n):
        def part(half, k):
            return lambda i: tensor[:, half, k * width + i * P:k * width + (i + 1) * P]
        return [(part(0, k), part(1, k)) for k in range(n)]

    def qk_tile(self, l, n, chunks, ready, dst, done_marks):
        slot, mark = yield from self.dense(("w_in", l, n), chunks, T1, ready)
        yield self.qk_norm(l, n, slot, mark, dst, done_marks)

    def qk_norm(self, l, n, slot, mark, dst, done_marks):
        dve = self.dve
        norm, norm_there = yield from self.norm_root()
        raw = yield from self.temps.get()
        copied = dve.do(lambda e: e.tensor_tensor(along(raw.ap[:, :], T1), across(slot.ap, T1), along(norm.ap[:, :], T1),
                                                  ALU.mult), mark, norm_there, raw.before)
        self.psum.give(slot, copied)
        yield
        sq, squared = yield from self.square(raw.ap[:, :], T1, copied)
        stat, mark = yield from self.sums(self.consts[:, C_BLOCK:C_BLOCK + P], [sq.ap], T1, [[squared, self.consts_there]])
        self.temps.give(sq, mark)
        root, there = yield from self.rsqrt_mean(stat, T1, HEAD_DIM, EPS, mark)
        gain = self.par(l, "q_g" if n < HEADS else "k_g")
        normed = dve.do(lambda e: e.scalar_tensor_tensor(raw.ap[:, :], raw.ap[:, :], gain, root.ap[:, :],
                                                         ALU.mult, ALU.mult), there, copied, self.params_there)
        self.temps.give(root, normed)
        yield
        rot, mark = yield from self.sums(self.consts[:, C_ROT16:C_ROT16 + P], [raw.ap], T1, [normed])
        done_marks[n] = yield from self.rotate(dst, raw, rot, T1, 0, normed, mark)

    def rotate(self, dst, raw, rot, width, table, there, mark):
        cos, sin = self.m["rope"][:, table, 0:width], self.m["rope"][:, table + 1, 0:width]
        a = self.pool.do(lambda e: e.tensor_tensor(dst, raw.ap[:, 0:width], cos, ALU.mult),
                         there, self.rope_there, self.arena_free)
        self.temps.give(raw, a, mark)
        tmp = yield from self.temps.get()
        b = self.dve.do(lambda e: e.tensor_tensor(along(tmp.ap[:, 0:width], width), across(rot.ap, width),
                                                  along(sin, width), ALU.mult), mark, tmp.before, self.rope_there)
        self.psum.give(rot, b)
        yield
        c = self.dve.do(lambda e: e.tensor_tensor(dst, dst, tmp.ap[:, 0:width], ALU.add), a, b)
        self.temps.give(tmp, c)
        yield
        return c

    def softmax_pair(self, scores, slots, probs, rows, keys, scale):
        dve, act = self.dve, self.act
        small = yield from self.small.get()
        top, total = small.ap[0:rows, 0:4], small.ap[0:rows, 4:8]
        marks = scores()
        yield
        if len(slots) == 1:
            both = slots[0].ap[0:rows, :].rearrange("p (b n) -> p b n", b=2)[:, :, 0:keys]
            there = dve.do(lambda e: e.reduce_max(top[:, 0:2], both, AX.X), marks, small.before)
            of = [slots[0].ap[0:rows, c * BANK:c * BANK + keys] for c in range(2)]
        else:
            of = [slots[c].ap[0:rows, 0:keys] for c in range(2)]
            for c in range(2):
                there = dve.do(lambda e: e.reduce_max(top[:, c:c + 1], of[c], AX.X), marks, small.before)
        yield
        there = dve.do(lambda e: e.tensor_scalar(top[:, 2:4], top[:, 0:2], -scale, None, ALU.mult), there)
        yield
        done = []
        for c in range(2):
            done.append(act.do(lambda e: e.activation(probs[c].ap[0:rows, 0:keys], of[c], ACT.Exp,
                                                      bias=top[:, 2 + c:3 + c], scale=scale,
                                                      accum_out=total[:, c:c + 1]), there, probs[c].before))
        for slot in slots:
            self.psum.give(slot, done[1])
        yield
        rates = dve.do(lambda e: e.reciprocal(total[:, 2:4], total[:, 0:2]), done)
        yield
        return small, total[:, 2:4], done, rates

    def diff_unit(self, l, h, i, q, k, v, there_yet, o_marks):
        pe, dve, act, m = self.pe, self.dve, self.act, self.m
        while there_yet(h) is None:
            yield
        inputs = there_yet(h)
        q0 = i * P
        rows = min(P, T1 - q0)
        keys = q0 + rows
        probs = yield from self.temps.get_all(2)
        slots = yield from self.psum.get_all(1 if keys <= BANK else 2)

        def scores():
            marks = []
            for c in range(2):
                slot, at = (slots[0], c * BANK) if keys <= BANK else (slots[c], 0)
                half = slice(c * HEAD_DIM, (c + 1) * HEAD_DIM)
                pe.wait(slot.before, inputs, self.masks_there)
                for k0, k1 in ((0, min(keys, BANK)), (BANK, keys)):
                    if k0 < k1:
                        pe.do(lambda e: e.matmul(slot.ap[0:rows, at + k0:at + k1], q[half, h, q0:q0 + rows],
                                                 k[half, h, k0:k1], start=True, stop=not k0 <= q0 < k1), signal=False)
                marks.append(pe.do(lambda e: e.matmul(slot.ap[0:rows, at + q0:at + keys], m["ident_big"][0:rows, 0:rows],
                                                      m["causal"][0:rows, 0:rows], start=False, stop=True)))
            return marks

        p1, p2 = probs
        small, rate, done, rates = yield from self.softmax_pair(scores, slots, probs, rows, keys, HEAD_DIM ** -0.5)
        a, b = p1.ap[0:rows, 0:keys], p2.ap[0:rows, 0:keys]
        scaled = self.pool.do(lambda e: e.tensor_scalar(a, a, rate[:, 0:1], None, ALU.mult), done, rates)
        there = dve.do(lambda e: e.tensor_tensor(rate[:, 1:2], rate[:, 1:2], m["lam"][0:rows, l, 5:6], ALU.mult), rates)
        yield
        there = dve.do(lambda e: e.scalar_tensor_tensor(a, b, rate[:, 1:2], a, ALU.mult, ALU.add), scaled, there, done)
        self.temps.give(p2, there)
        self.small.give(small, there)
        yield
        pt = yield from self.temps.get()
        slot = yield from self.psum.get()
        pe.wait(slot.before, there)
        blocks = [(j * P, min(P, keys - j * P)) for j in range(-(-keys // P))]
        for j, (k0, n) in enumerate(blocks):
            mark = pe.do(lambda e: e.transpose(slot.ap[0:n, j * rows:(j + 1) * rows], p1.ap[0:rows, k0:k0 + n],
                                               self.ident[0:rows, 0:rows]))
        self.temps.give(p1, mark)
        yield
        full = sum(n == P for _, n in blocks) * rows
        there = [act.do(lambda e: e.activation(pt.ap[:, 0:full], slot.ap[:, 0:full], ACT.Copy), mark, pt.before)]
        if blocks[-1][1] < P:
            n = blocks[-1][1]
            there.append(act.do(lambda e: e.activation(pt.ap[0:n, full:full + rows], slot.ap[0:n, full:full + rows],
                                                       ACT.Copy), mark))
        yield
        pe.wait(there)
        for j, (k0, n) in enumerate(blocks):
            mark = pe.do(lambda e: e.matmul(slot.ap[:, BANK:BANK + rows], v[0:n, j, h * P:(h + 1) * P],
                                            pt.ap[0:n, j * rows:(j + 1) * rows],
                                            start=j == 0, stop=j == len(blocks) - 1))
        self.temps.give(pt, mark)
        yield
        done = dve.do(lambda e: e.tensor_copy(q[:, h, q0:q0 + rows], slot.ap[:, BANK:BANK + rows]), mark)
        self.psum.give(slot, done, *there)
        o_marks[h].append(done)

    def recurrent_tile(self, l, n, slot, mark, gate, gates, gates_there, y, y_marks):
        m, dve, act, pool = self.m, self.dve, self.act, self.pool
        raw = y[:, n, :]
        norm, norm_there = yield from self.norm_root()
        nr = along(norm.ap[:, :], T1)
        there = dve.do(lambda e: e.tensor_tensor(along(raw, T1), across(slot.ap, T1), nr, ALU.mult), mark,
                       norm_there, self.arena_free)
        self.psum.give(slot, there)
        conv = yield from self.temps.get()
        xc = conv.ap
        w = lambda j: self.par(l, "conv_w", 4 * n + j)
        there = act.do(lambda e: e.activation(xc[:, :], raw, ACT.Identity, bias=self.par(l, "conv_b", n), scale=w(3)),
                       there, conv.before, self.params_there)
        yield
        for back in (1, 2, 3):
            there = dve.do(lambda e: e.scalar_tensor_tensor(
                xc[:, back:T1], raw[:, 0:T1 - back], w(3 - back), xc[:, back:T1], ALU.mult, ALU.add), there)
            yield
        conv_there = there
        half = yield from self.small.get()
        hb = half.ap
        there = dve.do(lambda e: e.tensor_scalar(hb[:, 0:1], self.par(l, "b_rg", n), 0.5, None, ALU.mult), half.before)
        half_there = dve.do(lambda e: e.tensor_scalar(hb[:, 1:2], self.par(l, "b_ig", n), 0.5, None, ALU.mult), there)
        tanhs = []
        for which in range(2):
            slot, mark = yield from self.sums(gates[:, which, n, :], [xc], T1, [[conv_there, gates_there]])
            tmp = yield from self.temps.get()
            there = act.do(lambda e: e.activation(
                along(tmp.ap[:, :], T1), across(slot.ap, T1), ACT.Tanh, bias=hb[:, which:which + 1], scale=0.5),
                mark, tmp.before, half_there)
            self.psum.give(slot, there)
            tanhs.append((tmp, there))
        self.small.give(half, there)
        (tr, r_there), (ti, i_there) = tanhs
        yield
        half_rate = m["lsig"][:, l, n:n + 1]
        while self.lsig_there[l] is None:
            yield
        rate_there = pool.do(lambda e: e.tensor_scalar(tr.ap[:, :], tr.ap[:, :], half_rate, half_rate,
                                                       ALU.mult, ALU.add), r_there, self.lsig_there[l])
        u_there = dve.do(lambda e: e.scalar_tensor_tensor(xc[:, :], ti.ap[:, :], 1.0, xc[:, :], ALU.add, ALU.mult),
                         i_there, mark)
        yield
        a_there = act.do(lambda e: e.activation(raw, tr.ap[:, :], ACT.Exp, scale=-1.0), rate_there, conv_there)
        w_there = act.do(lambda e: e.activation(tr.ap[:, :], tr.ap[:, :], ACT.Tanh, scale=0.5), rate_there)
        yield
        there = pool.do(lambda e: e.tensor_scalar(tr.ap[:, :], tr.ap[:, :], 0.0, None, ALU.max), w_there)
        yield
        there = act.do(lambda e: e.activation(tr.ap[:, :], tr.ap[:, :], ACT.Sqrt, scale=0.25), there)
        yield
        there = dve.do(lambda e: e.scalar_tensor_tensor(tr.ap[:, :], raw, 1.0, tr.ap[:, :], ALU.add, ALU.mult),
                       there, a_there)
        there = dve.do(lambda e: e.memset(tr.ap[:, 0:1], 0.5), there)
        yield
        there = pool.do(lambda e: e.tensor_tensor(xc[:, :], xc[:, :], tr.ap[:, :], ALU.mult), there, u_there)
        yield
        h_there = dve.do(lambda e: e.tensor_tensor_scan(ti.ap[:, :], raw, xc[:, :], 0.0, ALU.mult, ALU.add),
                         there, a_there, u_there)
        self.temps.give(conv, h_there)
        while not gate:
            yield
        gate_buf, gate_there = gate
        g = gate_buf.ap[:, :]
        there = act.do(lambda e: e.activation(tr.ap[:, :], g, ACT.Square), gate_there, there)
        yield
        there = pool.do(lambda e: e.tensor_scalar(tr.ap[:, :], tr.ap[:, :], 0.044715, 1.0, ALU.mult, ALU.add), there)
        yield
        there = pool.do(lambda e: e.tensor_tensor(tr.ap[:, :], tr.ap[:, :], g, ALU.mult), there)
        yield
        there = act.do(lambda e: e.activation(tr.ap[:, :], tr.ap[:, :], ACT.Tanh, scale=math.sqrt(2.0 / math.pi)),
                       there)
        yield
        there = dve.do(lambda e: e.scalar_tensor_tensor(g, tr.ap[:, :], 1.0, g, ALU.add, ALU.mult), there)
        self.temps.give(tr, there)
        yield
        there = dve.do(lambda e: e.scalar_tensor_tensor(raw, g, 0.5, ti.ap[:, :], ALU.mult, ALU.mult), there, h_there)
        self.temps.give(ti, there)
        self.temps.give(gate_buf, there)
        y_marks[n] = there
        yield

    def scaled_into_hid(self, src, root, gain, k, there, mixed):
        tmp = yield from self.temps.get()
        done = self.dve.do(lambda e: e.scalar_tensor_tensor(tmp.ap[:, :], src, gain, root.ap[:, :], ALU.mult, ALU.mult),
                           there, tmp.before)
        yield
        hi, lo = self.hid_chunk(k, T1)
        marks = yield from self.split_slowly(k, hi, lo, tmp.ap[:, :], done, self.hid_free)
        self.temps.give(tmp, *marks)
        mixed[k] = marks
        return done

    def sub_norm(self, l, h, q, o_marks, mixed):
        while len(o_marks[h]) < 5:
            yield
        sq, there = yield from self.square(q[:, h, :], T1, o_marks[h])
        stat, mark = yield from self.sums(self.m["ones"][:, :], [sq.ap], T1, [there])
        self.temps.give(sq, mark)
        root, there = yield from self.rsqrt_mean(stat, T1, P, EPS, mark)
        done = yield from self.scaled_into_hid(q[:, h, :], root, self.m["lam"][:, l, 6:7], h, there, mixed)
        self.temps.give(root, done)

    def recurrent_norm(self, l, y, y_marks, mixed):
        total = None
        for n in range(REC_TILES):
            while y_marks[n] is None:
                yield
            sq, there = yield from self.square(y[:, n, :], T1, y_marks[n])
            if total is None:
                total, total_there = sq, there
                continue
            total_there = self.pool.do(lambda e: e.tensor_tensor(total.ap[:, :], total.ap[:, :], sq.ap[:, :], ALU.add),
                                       total_there, there)
            self.temps.give(sq, total_there)
        stat, mark = yield from self.sums(self.m["ones"][:, :], [total.ap], T1, [total_there])
        self.temps.give(total, mark)
        root, there = yield from self.rsqrt_mean(stat, T1, REC_TILES * P, EPS, mark)
        for n in range(REC_TILES):
            done = yield from self.scaled_into_hid(y[:, n, :], root, self.par(l, "rec_g", n), HEADS + n, there, mixed)
        self.temps.give(root, done)

    def block1_layer(self, l, ready):
        m, pe, dve, act = self.m, self.pe, self.dve, self.act
        arena = m["arena"]
        q = arena[:, 0:4 * T1].rearrange("p (n t) -> p n t", n=4)
        k = arena[:, 4 * T1:8 * T1].rearrange("p (n t) -> p n t", n=4)
        y = arena[:, 8 * T1:12 * T1].rearrange("p (n t) -> p n t", n=4)
        v = arena[:, 12 * T1:12 * T1 + 5 * BANK].rearrange("p (n t) -> p n t", n=5)
        at = 12 * T1 + 5 * BANK
        gates = arena[:, at:at + 8 * P].rearrange("p (g n c) -> p g n c", g=2, n=4)
        gates_there = act.dma(gates, self.t["w_gates"][l], self.landing["landed_gates"], self.arena_free)
        at += 8 * P
        extra = [arena[:, at + n * T1:at + (n + 1) * T1] for n in range(5)] + [m["rope"][:, n, :] for n in (2, 3)]
        for ap in extra:
            self.temps.free.append(Buffer(ap))
            self.temps.free[-1].readers = list(self.arena_free)

        chunks = [self.act_chunk(c, T1) for c in range(DC)]
        qk_marks, v_marks = [None] * (2 * HEADS), []
        o_marks = [[] for _ in range(HEADS)]
        y_marks, mixed, root_read = [None] * REC_TILES, [None] * DC, []

        def there_yet(h):
            if qk_marks[h] is None or qk_marks[HEADS + h] is None or len(v_marks) < 5 or self.lam_there[l] is None:
                return None
            return [qk_marks[h], qk_marks[HEADS + h], *v_marks, self.lam_there[l]]

        def values():
            tokens = [(i, min(P, T1 - i * P)) for i in range(5)]
            factors, f_there = yield from self.token_factors(tokens)
            slots, mark = yield from self.values_token_major("w_v", (l,), self.token_chunks(m["act"], T1, DC),
                                                             [[r, self.pad_there] for r in ready], T1, HEADS * P)
            self.values_scaled(slots, mark, factors, f_there, tokens, v, v_marks)

        def recurrent(n):
            slot, mark = yield from self.dense(("w_in", l, 2 * HEADS + n), chunks, T1, ready)
            gate = []
            yield self.recurrent_tile(l, n, slot, mark, gate, gates, gates_there, y, y_marks)
            slot, mark = yield from self.dense(("w_in", l, 3 * HEADS + n), chunks, T1, ready)
            self.act_free = [mark]
            norm, norm_there = yield from self.norm_root()
            buf = yield from self.temps.get()
            there = dve.do(lambda e: e.tensor_tensor(along(buf.ap[:, :], T1), across(slot.ap, T1),
                                                     along(norm.ap[:, :], T1), ALU.mult), mark, norm_there, buf.before)
            self.psum.give(slot, there)
            root_read.append(there)
            gate += [buf, there]

        def products():
            for n in range(HEADS):
                yield from self.qk_tile(l, HEADS + n, chunks, ready, k[:, n, :], qk_marks)
                yield from self.qk_tile(l, n, chunks, ready, q[:, n, :], qk_marks)
                if n == 0:
                    yield from values()
                yield from recurrent(n)

        units = (self.diff_unit(l, h, i, q, k, v, there_yet, o_marks) for h in range(HEADS) for i in (4, 3, 2, 1, 0))
        norms = [self.sub_norm(l, h, q, o_marks, mixed) for h in range(HEADS)]
        once = [self.lambdas(l), self.log_sigmoid(l)] if l == 0 else []
        once += [self.lambdas(1), self.log_sigmoid(1)] if l == 0 else []
        together(products(), several(units, UNITS), several(norms, 2), self.recurrent_norm(l, y, y_marks, mixed),
                 several(once, 1))
        self.give_root(*root_read)
        self.arena_free = [mark for marks in mixed for mark in marks]
        mine = {id(ap) for ap in extra}
        for b in self.temps.free:
            if id(b.ap) in mine:
                self.arena_free += b.readers
        self.temps.free = [b for b in self.temps.free if id(b.ap) not in mine]
        assert len(self.temps.free) == TEMPS

        x = m["x"]
        ready = self.add_product("w_out", l, [self.hid_chunk(c, T1) for c in range(DC)], mixed, T1, x, 1.0,
                                 then=self.next_norm(lambda c: self.par(l, "ffn_g", c)))

        for f0, f1 in FF_GROUPS:
            hidden, root_read = [None] * (f1 - f0), []

            def up():
                for f in range(f0, f1):
                    g_slot, g_mark = yield from self.dense(("w_gu", l, f), chunks, T1, ready)
                    u_slot, u_mark = yield from self.dense(("w_gu", l, FF_TILES + f), chunks, T1, ready)
                    self.act_free = [u_mark]
                    if f == 0:
                        yield from self.norm_root()
                    yield self.swiglu(f - f0, g_slot, g_mark, u_slot, u_mark, hidden, root_read)
            beside = []
            if l == DEPTH - 1 and f0 == 0:
                self.rope_free = self.arena_free
                beside = [self.rope_tables2()]
            together(up(), *beside)
            then = None
            if f1 == FF_TILES:
                self.give_root(*root_read)
                then = (self.next_norm(lambda c: self.par(l + 1, "mix_g", c)) if l + 1 < DEPTH else self.block2_input)
            next_ready = self.add_product("w_down", l, [self.hid_chunk(c, T1) for c in range(f1 - f0)], hidden, T1, x,
                                          1.0, (f0, f1), then)
        return next_ready

    def values_scaled(self, slots, mark, factors, f_there, tokens, v, v_marks):
        act = self.act
        marks = []
        for i, rows in tokens:
            bank = slots[i // 2].ap[0:rows, (i % 2) * BANK:(i % 2 + 1) * BANK]
            marks.append(act.do(lambda e: e.activation(v[0:rows, i, :], bank, ACT.Copy,
                                                       scale=factors.ap[0:rows, i:i + 1]),
                                mark, self.arena_free, f_there))
        self.small.give(factors, marks[-1])
        for s in slots:
            self.psum.give(s, marks[-1])
        v_marks += marks

    def token_factors(self, tokens):
        pe, act = self.pe, self.act
        norm, norm_there = yield from self.norm_root()
        stat = yield from self.psum.get()
        pe.wait(stat.before, norm_there)
        for i, rows in tokens:
            turned = pe.do(lambda e: e.matmul(stat.ap[0:rows, i:i + 1], norm.ap[:, i * P:i * P + rows],
                                              self.ident[:, 0:1], start=True, stop=True))
        factors = yield from self.small.get()
        for i, rows in tokens:
            f_there = act.do(lambda e: e.activation(factors.ap[0:rows, i:i + 1], stat.ap[0:rows, i:i + 1], ACT.Copy),
                             turned, factors.before)
        self.psum.give(stat, f_there)
        yield
        return factors, f_there

    def next_norm(self, g):
        def then(k, there, ready):
            ready[k] = self.next_input(k, g(k), T1, there, self.act_free)
            yield
            yield from self.add_square(k, there)
        return then

    def block2_input(self, k, there, ready):
        ready[k] = self.next_input(k, None, T2, there, self.act_free)
        yield

    def swiglu(self, at, g_slot, g_mark, u_slot, u_mark, hidden, root_read):
        norm, norm_there = yield from self.norm_root()
        nr = along(norm.ap[:, :], T1)
        a, b = yield from self.temps.get_all(2)
        g, u = a.ap[:, :], b.ap[:, :]
        dve = self.dve
        there = dve.do(lambda e: e.tensor_tensor(along(g, T1), across(g_slot.ap, T1), nr, ALU.mult),
                       g_mark, norm_there, a.before)
        self.psum.give(g_slot, there)
        yield
        th = self.act.do(lambda e: e.activation(u, g, ACT.Tanh, scale=0.5), there, b.before)
        yield
        there = dve.do(lambda e: e.scalar_tensor_tensor(g, u, 1.0, g, ALU.add, ALU.mult), th)
        u_there = dve.do(lambda e: e.scalar_tensor_tensor(along(u, T1), across(u_slot.ap, T1), 0.5, nr, ALU.mult,
                                                          ALU.mult), there, u_mark)
        self.psum.give(u_slot, u_there)
        root_read[:] = [u_there]
        yield
        there = dve.do(lambda e: e.tensor_tensor(g, g, u, ALU.mult), u_there)
        self.temps.give(b, there)
        yield
        hi, lo = self.hid_chunk(at, T1)
        a_mark = self.act.do(lambda e: e.activation(hi, g, ACT.Copy), there, self.hid_free)
        yield
        b_mark = dve.do(lambda e: e.tensor_tensor(lo, g, hi.bitcast(F32), ALU.subtract), a_mark)
        self.temps.give(a, a_mark, b_mark)
        hidden[at] = [a_mark, b_mark]

    def add_product(self, name, l, chunks, ready, width, x, alpha, ks=None, then=None):
        marks = [None] * DC

        def add(n, slot, mark):
            done = self.dve.do(lambda e: e.scalar_tensor_tensor(
                along(x[:, n, :], width), along(x[:, n, :], width), alpha, across(slot.ap, width), ALU.mult, ALU.add),
                mark, self.x_marks[n])
            self.psum.give(slot, done)
            self.x_marks[n] = marks[n] = [done]
            yield
            if then is not None:
                yield from then(n, done, marks)

        def tiles():
            for n in range(DC):
                key = (name, l, n) if ks is None else (name, l, n, *ks)
                slot, mark = yield from self.dense(key, chunks, width, ready)
                yield add(n, slot, mark)
            if name == "w_mo":
                self.act_free = [mark]
            else:
                self.hid_free = [mark]
        together(tiles())
        return marks


    def rope_tables2(self):
        m, dve, act = self.m, self.dve, self.act
        pos_i, pos, ang, turns = yield from self.temps.get_all(4)
        landed = self.act.dma(pos_i.ap[:, 0:T2].bitcast(I32), self.t["positions"], self.landing["landed_positions"],
                              pos_i.before)
        pos_there = dve.do(lambda e: e.tensor_copy(pos.ap[:, 0:T2], pos_i.ap[:, 0:T2].bitcast(I32)), landed, pos.before)
        self.temps.give(pos_i, pos_there)
        two_pi = 2.0 * math.pi
        part1 = 6.28125
        part2 = float(np.float32(np.round((two_pi - part1) * 2.0 ** 21) / 2.0 ** 21))
        part3 = float(np.float32(two_pi - part1 - part2))
        magic = 1.5 * 2.0 ** 23
        a, n = ang.ap[:, 0:T2], turns.ap[:, 0:T2]
        there = [ang.before, turns.before]
        for kind in range(2):
            inv = self.consts[:, C_INV + kind:C_INV + kind + 1]
            for table, shift in ((2 * kind, 0.25), (2 * kind + 1, 0.0)):
                there = dve.do(lambda e: e.tensor_scalar(a, pos.ap[:, 0:T2], inv, None, ALU.mult),
                               pos_there, self.consts_there, there)
                yield
                there = dve.do(lambda e: e.tensor_scalar(n, a, 1.0 / two_pi, shift, ALU.mult, ALU.add), there)
                yield
                there = dve.do(lambda e: e.tensor_scalar(n, n, magic, None, ALU.add), there)
                yield
                there = dve.do(lambda e: e.tensor_scalar(n, n, magic, None, ALU.subtract), there)
                for part in (part1, part2, part3):
                    yield
                    there = dve.do(lambda e: e.scalar_tensor_tensor(a, n, -part, a, ALU.mult, ALU.add), there)
                yield
                there = dve.do(lambda e: e.tensor_scalar(a, a, shift * two_pi, 3.1415925, ALU.add, ALU.min),
                               there)
                yield
                there = dve.do(lambda e: e.tensor_scalar(a, a, -3.1415925, None, ALU.max), there)
                yield
                there = act.do(lambda e: e.activation(m["rope"][:, table, 0:T2], a, ACT.Sin),
                               there, self.rope_free)
        self.temps.give(pos, there)
        self.temps.give(ang, there)
        self.temps.give(turns, there)
        self.rope_there = there

    def tile2(self, l, tile, chunks, ready, dst, marks):
        slot, mark = yield from self.dense(("w_in2", l, SLOT2[tile]), chunks, T2, ready)
        self.act_free = [mark]
        yield self.tile2_out(tile, slot, mark, dst, marks)

    def tile2_out(self, tile, slot, mark, dst, marks):
        kind, _ = tile
        scale = HEAD_DIM ** -0.5 if kind in ("cq", "dq") else 1.0
        if kind in ("cb", "cc", "ch", "cq", "ck"):
            done = self.act.do(lambda e: e.activation(dst, slot.ap[:, 0:T2], ACT.Copy, scale=scale),
                               mark, self.arena_free)
            self.psum.give(slot, done)
            marks[tile] = done
            return
        raw = yield from self.temps.get()
        copied = self.act.do(lambda e: e.activation(raw.ap[:, 0:T2], slot.ap[:, 0:T2], ACT.Copy, scale=scale),
                             mark, raw.before)
        self.psum.give(slot, copied)
        yield
        at, table = (C_ROT16, 0) if kind in ("dq", "dk") else (C_ROT8, 2)
        rot, mark = yield from self.sums(self.consts[:, at:at + P], [raw.ap], T2, [copied])
        marks[tile] = yield from self.rotate(dst, raw, rot, T2, table, copied, mark)

    def index_scores(self, i, A, marks, found):
        pe, dve, act = self.pe, self.dve, self.act
        needed = [("iq", 0), ("iq", 1), ("ik", 0), "iw"]
        while any(n not in marks for n in needed):
            yield
        q0, keys = i * P, (i + 1) * P
        acc = yield from self.temps.get()
        before = acc.before
        for h in range(IDX_HEADS):
            rows = slice(IDX_DIM * (h % 4), IDX_DIM * (h % 4 + 1))
            tmp = yield from self.temps.get()
            slot = yield from self.psum.get()
            mark = pe.do(lambda e: e.matmul(
                slot.ap[:, 0:keys], A("iq", h // 4)[rows, q0:q0 + P], A("ik", 0)[rows, 0:keys], start=True, stop=True),
                slot.before, [marks[n] for n in needed])
            yield
            there = act.do(lambda e: e.activation(tmp.ap[:, 0:keys], slot.ap[:, 0:keys], ACT.Relu), mark, tmp.before)
            self.psum.give(slot, there)
            yield
            weight = self.m["iw"][:, i, h:h + 1]
            if h == 0:
                done = dve.do(lambda e: e.tensor_scalar(acc.ap[:, 0:keys], tmp.ap[:, 0:keys], weight, None, ALU.mult),
                              there, before, marks["iw"])
            else:
                done = dve.do(lambda e: e.scalar_tensor_tensor(
                    acc.ap[:, 0:keys], tmp.ap[:, 0:keys], weight, acc.ap[:, 0:keys], ALU.mult, ALU.add), there, done)
            self.temps.give(tmp, done)
            yield
        done = dve.do(lambda e: e.memset(acc.ap[0:CHUNK, keys - CHUNK:keys], INADMISSIBLE), done)
        found[i] = (acc, done)

    def top_keys(self, i, A, marks, select_marks):
        dve, found = self.dve, {}
        yield from self.index_scores(i, A, marks, found)
        acc, there = found[i]
        keys = (i + 1) * P
        best = yield from self.small.get()
        s = acc.ap[:, 0:keys]
        dve.wait(best.before)
        for _ in range(TOPK // 8):
            there = dve.do(lambda e: e.max(best.ap[:, 0:8], s), there)
            yield
            there = dve.do(lambda e: e.match_replace(s, best.ap[:, 0:8], s, TAKEN), there)
            yield
        self.small.give(best, there)
        there = dve.do(lambda e: e.tensor_scalar(self.m["select"][:, i, 0:keys], s, TAKEN, 1.0,
                                                 ALU.is_equal, ALU.subtract), there, self.select_free)
        self.temps.give(acc, there)
        select_marks[i] = there

    def pair_unit(self, i, q, k, value, bias, inputs, mix_at, mixed):
        pe, dve, act, m = self.pe, self.dve, self.act, self.m
        while inputs() is None:
            yield
        there = inputs()
        q0, keys = i * P, (i + 1) * P
        probs = yield from self.temps.get_all(2)
        slot = yield from self.psum.get()

        def scores():
            pe.wait(slot.before, there, self.masks_there)
            for c in range(2):
                half = slice(c * HEAD_DIM, (c + 1) * HEAD_DIM)
                at = c * BANK
                pe.do(lambda e: e.matmul(slot.ap[:, at:at + keys], q[half, q0:q0 + P], k[half, 0:keys],
                                         start=True, stop=False), signal=False)
                if bias is None:
                    mark = pe.do(lambda e: e.matmul(slot.ap[:, at:at + keys], m["ident_big"][:, :],
                                                    m["select"][:, i, 0:keys], start=False, stop=True))
                else:
                    near = min(keys, 2 * P)
                    mark = pe.do(lambda e: e.matmul(slot.ap[:, at + keys - near:at + keys], self.ident,
                                                    bias[c].ap[0][:, 256 - near:256], start=False, stop=True))
            return [mark]

        small, rate, done, rates = yield from self.softmax_pair(scores, [slot], probs, P, keys, 1.0)
        ready = []
        for c in range(2):
            p = probs[c].ap[:, 0:keys]
            ready.append(self.pool.do(lambda e: e.tensor_scalar(p, p, rate[:, c:c + 1], None, ALU.mult), done, rates))
        self.small.give(small, *ready)
        yield
        slot = yield from self.psum.get()
        pe.wait(slot.before)
        pts = []
        for c in range(2):
            pe.wait(ready[c])
            for j in range(i + 1):
                mark = pe.do(lambda e: e.transpose(slot.ap[:, c * BANK + j * P:c * BANK + (j + 1) * P],
                                                   probs[c].ap[:, j * P:(j + 1) * P], self.ident))
            self.temps.give(probs[c], mark)
            yield
            pt = yield from self.temps.get()
            there = act.do(lambda e: e.activation(pt.ap[:, 0:keys], slot.ap[:, c * BANK:c * BANK + keys],
                                                  ACT.Copy), mark, pt.before)
            pts.append((pt, there))
        yield
        for c, (pt, there) in enumerate(pts):
            pe.wait(there)
            for j in range(i + 1):
                mark = pe.do(lambda e: e.matmul(
                    slot.ap[c * HEAD_DIM:(c + 1) * HEAD_DIM, c * BANK:c * BANK + P], value(c, j),
                    pt.ap[:, j * P:(j + 1) * P], start=j == 0, stop=j == i))
            self.temps.give(pt, mark)
        yield
        hi, lo = self.hid_chunk(mix_at, T2)
        tops, rests = [], []
        for c in range(2):
            rows = slice(c * HEAD_DIM, (c + 1) * HEAD_DIM)
            tops.append(act.do(lambda e: e.activation(hi[rows, q0:q0 + P], slot.ap[rows, c * BANK:c * BANK + P],
                                                      ACT.Copy), mark, self.hid_free))
        yield
        for c in range(2):
            rows = slice(c * HEAD_DIM, (c + 1) * HEAD_DIM)
            rests.append(dve.do(lambda e: e.tensor_tensor(lo[rows, q0:q0 + P], slot.ap[rows, c * BANK:c * BANK + P],
                                                          hi[rows, q0:q0 + P].bitcast(F32), ALU.subtract),
                                tops, mark))
        self.psum.give(slot, *tops, *rests)
        mixed[mix_at] += tops + rests

    def load_bias(self, l, h):
        buf = yield from self.biases.get()
        ap, landing = buf.ap
        landed = self.sp.dma(ap[:, :], self.t["rel_bias"][l, h], self.landing[landing], buf.before)
        far = yield from self.small.get()
        there = self.dve.do(lambda e: e.tensor_copy(far.ap[:, 0:1], ap[:, 0:1]), landed, far.before)
        there = self.dve.do(lambda e: e.tensor_scalar(ap[:, :], ap[:, :], far.ap[:, 0:1], None, ALU.subtract), there)
        self.small.give(far, there)
        yield
        there = self.dve.do(lambda e: e.memset(ap[0:CHUNK, 256 - CHUNK:256], -MASKED), there)
        return buf, there

    def chunk_attention(self, l, A, tok, marks, mixed):
        for p in range(CHK_PAIRS):
            bufs, there = [], []
            for c in range(2):
                buf, mark = yield from self.load_bias(l, 2 * p + c)
                bufs.append(buf)
                there.append(mark)

            def inputs():
                if ("cq", p) in marks and ("ck", p) in marks and "iw" in marks:
                    return [marks[("cq", p)], marks[("ck", p)], marks["tok"], there]
                return None

            def value(c, j):
                at = TOK_V_CHK + (2 * p + c) * HEAD_DIM
                return tok[:, j, at:at + HEAD_DIM]
            yield from several((self.pair_unit(i, A("cq", p), A("ck", p), value, bufs, inputs, 5 + p, mixed)
                                for i in (3, 2, 1, 0)), 2)
            for buf in bufs:
                self.biases.give(buf, (self.pe.sem, self.pe.count))

    def selected_attention(self, A, tok, marks, select_marks, mixed):
        def unit(p, i):
            def inputs():
                if ("dq", p) in marks and ("dk", 0) in marks and i in select_marks:
                    return [marks[("dq", p)], marks[("dk", 0)], marks["tok"], select_marks[i]]
                return None
            return self.pair_unit(i, A("dq", p), A("dk", 0), lambda c, j: tok[:, j, TOK_V_DSA:TOK_V_DSA + HEAD_DIM],
                                  None, inputs, 2 + p, mixed)
        return several((unit(p, i) for p in range(DSA_PAIRS) for i in range(4)), 2)

    def convolution(self, l, n, A, marks, mixed, conv_done):
        while any((kind, n) not in marks for kind in ("cb", "cc", "ch")):
            yield
        dve = self.dve
        u, y = yield from self.temps.get_all(2)
        w = lambda j: self.par(l, "conv_w2", 3 * n + j)
        there = self.pool.do(lambda e: e.tensor_tensor(u.ap[:, 0:T2], A("cc", n), A("ch", n), ALU.mult),
                             marks[("cc", n)], marks[("ch", n)], u.before)
        yield
        there = self.act.do(lambda e: e.activation(y.ap[:, 0:T2], u.ap[:, 0:T2], ACT.Copy, scale=w(2)), there, y.before)
        yield
        for back in (1, 2):
            there = dve.do(lambda e: e.scalar_tensor_tensor(
                y.ap[:, back:T2], u.ap[:, 0:T2 - back], w(2 - back), y.ap[:, back:T2], ALU.mult, ALU.add), there)
            yield
        self.temps.give(u, there)
        there = self.pool.do(lambda e: e.tensor_tensor(y.ap[:, 0:T2], y.ap[:, 0:T2], A("cb", n), ALU.mult), there,
                             marks[("cb", n)])
        conv_done.append(there)
        yield
        hi, lo = self.hid_chunk(n, T2)
        mixed[n] = yield from self.split_slowly(n, hi, lo, y.ap[:, 0:T2], there, self.hid_free)
        self.temps.give(y, *mixed[n])

    def load_memory(self, ready):
        m = self.m
        free = self.act_free
        for n in range(DC // 2):
            buf = yield from self.temps.get()
            at = n * 2 * MEM
            landed = self.sp.dma(buf.ap[:, 0:2 * MEM], self.t["mem_t"][:, at:at + 2 * MEM],
                                 self.landing[f"landed_mem{n}"], buf.before)
            there = self.split_into(m["act"][:, 0, at:at + 2 * MEM], m["act"][:, 1, at:at + 2 * MEM],
                                    buf.ap[:, 0:2 * MEM], landed, free)
            self.temps.give(buf, *there)
            ready += [there, there]
            yield

    def memory_keys(self, l, ready, kT, marks):
        chunks = [self.act_chunk(c, MEM) for c in range(DC)]

        def out(n, slot, mark):
            done = self.act.do(lambda e: e.activation(kT[:, n, :], slot.ap[:, 0:MEM], ACT.Copy), mark, self.mem_free)
            self.psum.give(slot, done)
            marks.append(done)
            yield
        for n in range(DC):
            slot, mark = yield from self.dense(("w_mk", l, n), chunks, MEM, ready)
            self.act_free = [mark]
            yield out(n, slot, mark)

    def memory_values(self, l, ready, v, marks):
        for half in range(2):
            slots, mark = yield from self.values_token_major("w_mv", (l, half), self.token_chunks(self.m["act"], MEM, DC),
                                                             ready, MEM, BANK)
            for i in range(2):
                done = self.act.do(lambda e: e.activation(v[i][:, half * BANK:(half + 1) * BANK],
                                                          slots[0].ap[:, i * BANK:(i + 1) * BANK], ACT.Copy),
                                   mark, self.mem_free)
                marks.append(done)
            self.psum.give(slots[0], done)
            yield

    def memory_unit(self, h, i, q, kT, v, q_marks, mem_marks, mixed):
        pe, dve, act = self.pe, self.dve, self.act
        while q_marks[2 * h] is None or q_marks[2 * h + 1] is None:
            yield
        q0, scale = i * P, MEM_DIM ** -0.5
        slot = yield from self.psum.get()
        top = yield from self.small.get()
        prob = yield from self.temps.get()
        pe.wait(slot.before, mem_marks)
        for c in range(2):
            mark = pe.do(lambda e: e.matmul(slot.ap[:, 0:MEM], q[:, 2 * h + c, q0:q0 + P], kT[:, 2 * h + c, :],
                                            start=c == 0, stop=c == 1), q_marks[2 * h + c])
        yield
        there = dve.do(lambda e: e.reduce_max(top.ap[:, 0:1], slot.ap[:, 0:MEM], AX.X), mark, top.before)
        yield
        there = dve.do(lambda e: e.tensor_scalar(top.ap[:, 1:2], top.ap[:, 0:1], -scale, None, ALU.mult), there)
        yield
        done = act.do(lambda e: e.activation(prob.ap[:, 0:MEM], slot.ap[:, 0:MEM], ACT.Exp, bias=top.ap[:, 1:2],
                                             scale=scale, accum_out=top.ap[:, 2:3]), there, prob.before)
        self.psum.give(slot, done)
        yield
        there = dve.do(lambda e: e.reciprocal(top.ap[:, 3:4], top.ap[:, 2:3]), done)
        yield
        there = self.pool.do(lambda e: e.tensor_scalar(prob.ap[:, 0:MEM], prob.ap[:, 0:MEM], top.ap[:, 3:4], None,
                                                       ALU.mult), done, there)
        self.small.give(top, there)
        yield
        pt = yield from self.temps.get()
        slot = yield from self.psum.get()
        pe.wait(slot.before, there)
        for j in range(2):
            mark = pe.do(lambda e: e.transpose(slot.ap[:, j * P:(j + 1) * P], prob.ap[:, j * P:(j + 1) * P], self.ident))
        self.temps.give(prob, mark)
        yield
        there = act.do(lambda e: e.activation(pt.ap[:, 0:MEM], slot.ap[:, 0:MEM], ACT.Copy), mark, pt.before)
        yield
        pe.wait(there)
        for c in range(2):
            for j in range(2):
                mark = pe.do(lambda e: e.matmul(
                    slot.ap[:, BANK + c * P:BANK + (c + 1) * P], v[j][:, (2 * h + c) * P:(2 * h + c + 1) * P],
                    pt.ap[:, j * P:(j + 1) * P], start=j == 0, stop=j == 1))
        self.temps.give(pt, mark)
        yield
        view = lambda half: self.m["act"][:, half, 2 * h * T2:(2 * h + 2) * T2].rearrange(
            "p (c t) -> p c t", c=2)[:, :, q0:q0 + P]
        src = slot.ap[:, BANK:BANK + 2 * P].rearrange("p (c t) -> p c t", c=2)
        a = act.do(lambda e: e.activation(view(0), src, ACT.Copy), mark, self.act_free)
        yield
        b = dve.do(lambda e: e.tensor_tensor(view(1), src, view(0).bitcast(F32), ALU.subtract), a, mark)
        self.psum.give(slot, a, b, there)
        mixed[2 * h] += [a, b]
        mixed[2 * h + 1] += [a, b]

    def block2_layer(self, l, ready, last):
        m, pe, dve, act = self.m, self.pe, self.dve, self.act
        arena = m["arena"]
        x = m["x"][:, :, META:T1]

        def A(kind, n):
            at = SLOT2[(kind, n)]
            return arena[:, at * T2:(at + 1) * T2]

        tok0 = len(TILES2) * T2
        tok = arena[:, tok0:tok0 + 4 * TOK_COLS].rearrange("p (i c) -> p i c", i=4)
        chunks = [self.act_chunk(c, T2) for c in range(DC)]
        marks, select_marks = {}, {0: self.masks_there}
        mixed = [[] for _ in range(DC)]
        conv_done, mem_ready, mem_marks = [], [], []
        base = SLOT2[("cb", 0)] * T2
        kT = arena[:, base:base + DC * MEM].rearrange("p (n t) -> p n t", n=DC)
        v = [arena[:, base + DC * MEM:base + DC * MEM + D], arena[:, tok0 + 4 * TOK_COLS:tok0 + 4 * TOK_COLS + D]]

        def token_major():
            slots, mark = yield from self.values_token_major("w_tok", (l,), self.token_chunks(m["act"], T2, DC), ready,
                                                             T2, TOK_COLS)
            for i in range(4):
                bank = slots[i // 2].ap[:, (i % 2) * BANK:(i % 2) * BANK + TOK_COLS]
                marks["tok"] = act.do(lambda e: e.activation(tok[:, i, :], bank, ACT.Copy), mark, self.arena_free)
            for s in slots:
                self.psum.give(s, marks["tok"])
            yield
            for i in range(4):
                done = dve.do(lambda e: e.tensor_scalar(m["iw"][:, i, :], tok[:, i, TOK_IW:TOK_COLS],
                                                        IDX_HEADS ** -0.5, None, ALU.mult), marks["tok"])
            marks["iw"] = done

        def products():
            for tile in (("iq", 0), ("iq", 1), ("ik", 0)):
                yield from self.tile2(l, tile, chunks, ready, A(*tile), marks)
            yield from token_major()
            rest = [(kind, n) for n in range(3) for kind in ("cq", "ck")]
            rest += [(kind, n) for n in range(2) for kind in ("cb", "cc", "ch")]
            rest += [("dk", 0)] + [("dq", n) for n in range(3)]
            for tile in rest:
                yield from self.tile2(l, tile, chunks, ready, A(*tile), marks)
            yield from self.load_memory(mem_ready)
            while len(conv_done) < CONV_TILES:
                yield
            self.mem_free = conv_done
            yield from self.memory_values(l, mem_ready, v, mem_marks)

        together(products(), self.top_keys(1, A, marks, select_marks), self.top_keys(2, A, marks, select_marks),
                 self.top_keys(3, A, marks, select_marks), self.chunk_attention(l, A, tok, marks, mixed),
                 several((self.convolution(l, n, A, marks, mixed, conv_done) for n in range(CONV_TILES)), 1),
                 self.selected_attention(A, tok, marks, select_marks, mixed))
        self.select_free = [(pe.sem, pe.count)]
        self.arena_free = [(pe.sem, pe.count)]

        hid = [self.hid_chunk(c, T2) for c in range(DC)]
        ready = [None] * DC
        def mix_and_keys():
            yield from self.normed_product("w_mix", l, hid, mixed, ALPHA, None, lambda c: self.par(l, "ln1_g", c),
                                           lambda c: self.par(l, "ln1_b", c), self.hid_chunk, lambda: self.hid_free,
                                           ready)
            yield from self.memory_keys(l, mem_ready, kT, mem_marks)
        together(mix_and_keys())

        qbase = SLOT2[("cq", 0)] * T2
        q = arena[:, qbase:qbase + DC * T2].rearrange("p (n t) -> p n t", n=DC)
        q_marks = [None] * DC
        mixed = [[] for _ in range(DC)]

        def q_out(n, slot, mark):
            q_marks[n] = act.do(lambda e: e.activation(q[:, n, :], slot.ap[:, 0:T2], ACT.Copy), mark, self.arena_free)
            self.psum.give(slot, q_marks[n])
            yield

        def queries():
            first = yield from self.dense_together([("w_mq", l, n) for n in (0, 1)], hid, T2, ready)
            for n in range(DC):
                slot, mark = first.pop(0) if first else (yield from self.dense(("w_mq", l, n), hid, T2, ready))
                self.hid_free = [mark]
                yield q_out(n, slot, mark)
        together(queries(), several((self.memory_unit(h, i, q, kT, v, q_marks, mem_marks, mixed)
                                     for h in range(MEM_HEADS) for i in range(4)), 4))
        self.arena_free = [(pe.sem, pe.count)]
        ready = [None] * DC
        together(self.normed_product("w_mo", l, chunks, mixed, ALPHA, None, lambda c: self.par(l, "ln2_g", c),
                                     lambda c: self.par(l, "ln2_b", c), self.act_chunk, lambda: self.act_free, ready))

        for f0, f1 in FF2_GROUPS:
            hidden = [None] * (f1 - f0)

            def up():
                first = []
                if f0 == 0:
                    first = yield from self.dense_together([("w_ff1", l, f) for f in (0, 1)], chunks, T2, ready)
                for f in range(f0, f1):
                    slot, mark = first.pop(0) if first else (yield from self.dense(("w_ff1", l, f), chunks, T2, ready))
                    self.act_free = [mark]
                    yield self.squared_relu(f - f0, slot, mark, hidden)
            together(up())
            if f1 < FF2_TILES:
                self.add_product("w_ff2", l, hid[0:f1 - f0], hidden, T2, x, ALPHA if f0 == 0 else 1.0, (f0, f1))
        ready = [None] * DC
        together(self.normed_product("w_ff2", l, hid, hidden, 1.0, (f0, f1), lambda c: self.par(l, "ln3_g", c),
                                     lambda c: self.par(l, "ln3_b", c), None if last else self.act_chunk,
                                     lambda: self.act_free, ready))
        return ready

    def squared_relu(self, at, slot, mark, hidden):
        tmp = yield from self.temps.get()
        ap = tmp.ap[:, 0:T2]
        there = self.act.do(lambda e: e.activation(ap, slot.ap[:, 0:T2], ACT.Relu), mark, tmp.before)
        self.psum.give(slot, there)
        yield
        there = self.act.do(lambda e: e.activation(ap, ap, ACT.Square), there)
        yield
        hi, lo = self.hid_chunk(at, T2)
        a = self.act.do(lambda e: e.activation(hi, ap, ACT.Copy), there, self.hid_free)
        yield
        b = self.dve.do(lambda e: e.tensor_tensor(lo, ap, hi.bitcast(F32), ALU.subtract), a)
        self.temps.give(tmp, a, b)
        hidden[at] = [a, b]


    def write(self):
        m = self.m
        self.arena_free, self.hid_free, self.select_free = [], [], []
        self.act_free = []
        self.start()
        self.rope_there = self.consts_there
        landed = [self.x_landed[c // (DC // 2)] for c in range(DC)]
        self.x_marks = [[mark] for mark in landed]
        self.root = None
        ready = [None] * DC
        then = self.next_norm(lambda c: self.par(0, "mix_g", c))
        together(*(then(c, landed[c], ready) for c in range(DC)))
        for l in range(DEPTH):
            ready = self.block1_layer(l, ready)
        x = m["x"][:, :, META:T1]
        for l in range(DEPTH):
            ready = self.block2_layer(l, ready, l == DEPTH - 1)
        for c in range(DC):
            stored = self.sp.dma(self.out[:, c, :], x[:, c, :], self.landing["stored_out"], ready[c])
        self.sp.wait(stored)



def constants():
    c = np.zeros((P, C_COLS), np.float32)
    c[:, C_IDENT:C_IDENT + P] = np.eye(P)
    c[:, C_BLOCK:C_BLOCK + P] = np.kron(np.eye(2), np.ones((HEAD_DIM, HEAD_DIM)))

    def partner(head, half):
        r = np.zeros((P, P))
        for p in range(P):
            d = p % head
            if d < half:
                r[p + half, p] = -1.0
            elif d < 2 * half:
                r[p - half, p] = 1.0
        return r

    c[:, C_ROT16:C_ROT16 + P] = partner(HEAD_DIM, 8)
    c[:, C_ROT8:C_ROT8 + P] = partner(IDX_DIM, 4)
    q, k = np.arange(P)[:, None], np.arange(P)[None, :]
    c[:, C_CAUSAL:C_CAUSAL + P] = -1.0 * (k > q)
    c[:, C_CHUNK:C_CHUNK + P] = -1.0 * (k // CHUNK > q // CHUNK)

    def inverse(head, half):
        freq = np.float32(ROPE_THETA) ** (-np.arange(half, dtype=np.float32) / np.float32(half))
        col = np.zeros(P, np.float32)
        for p in range(P):
            d = p % head
            if d < 2 * half:
                col[p] = freq[d % half]
        return col

    inv = inverse(HEAD_DIM, 8)
    c[:, C_INV] = inv
    c[:, C_INV + 1] = inverse(IDX_DIM, 4)
    ang = np.arange(T1, dtype=np.float32)[None, :] * inv[:, None]
    c[:, C_COS1:C_COS1 + T1] = np.cos(ang.astype(np.float64))
    c[:, C_SIN1:C_SIN1 + T1] = np.sin(ang.astype(np.float64))
    return c


def columns_of_block2():
    widths = [("cb", 256), ("cc", 256), ("ch", 256), ("dq", 384), ("dk", 64), ("dv", 64), ("iq", 256),
              ("ik", 32), ("iw", 8), ("cq", 384), ("ck", 384), ("cv", 384)]
    at, start = 0, {}
    for name, n in widths:
        start[name] = at
        at += n
    tiles = []
    for kind, n in TILES2:
        if kind == "dk":
            tiles.append(np.tile(start["dk"] + np.arange(64), 2))
        elif kind == "ik":
            tiles.append(np.tile(start["ik"] + np.arange(32), 4))
        else:
            tiles.append(start[kind] + n * P + np.arange(P))
    tok = np.concatenate([start["cv"] + np.arange(384), start["dv"] + np.arange(64), start["iw"] + np.arange(8)])
    return np.concatenate(tiles), tok


def by_tiles(w):
    L, K, N = w.shape
    return np.ascontiguousarray(w.reshape(L, K // P, P, N // P, P).transpose(0, 3, 2, 1, 4).reshape(L, N // P, P, K))


def by_chunks(w, per):
    L, K, N = w.shape
    g = K // P // per
    return np.ascontiguousarray(w.reshape(L, g, per, P, N).transpose(0, 1, 3, 2, 4).reshape(L, g, P, per * N))


def feature_major(x):
    return np.ascontiguousarray(x.T.reshape(-1, P, x.shape[0]).transpose(1, 0, 2))


def per_partition(v):
    return v.reshape(DEPTH, -1, P)


def layout(a):
    t = {}
    t["x_t"] = feature_major(a["x"][0])
    t["meta_t"] = feature_major(a["meta_tokens"])
    t["mem_t"] = feature_major(a["mem_2"][0]).reshape(P, DC * MEM)
    t["positions"] = np.ascontiguousarray(np.broadcast_to(a["positions_2"], (P, T2)))
    w = a["w_in"]
    t["w_in"] = by_tiles(np.concatenate([w[:, :, 0:1024], w[:, :, 1536:2560]], axis=2))
    t["w_v"] = by_chunks(w[:, :, 1024:1536], 2)
    t["w_out"] = by_tiles(a["w_out"])
    t["w_gu"] = by_tiles(a["w_gu"])
    t["w_down"] = by_tiles(a["w_down"])
    feature, token = columns_of_block2()
    t["w_in2"] = by_tiles(a["w_in_2"][:, :, feature])
    t["w_tok"] = by_chunks(a["w_in_2"][:, :, token], 2)
    t["w_mix"] = by_tiles(a["w_mix_out_2"])
    t["w_mq"] = by_tiles(a["w_mq_2"])
    t["w_mk"] = by_tiles(a["w_mkv_2"][:, :, 0:D])
    t["w_mv"] = np.stack([by_chunks(a["w_mkv_2"][:, :, D + h * BANK:D + (h + 1) * BANK], 2) for h in range(2)], axis=1)
    t["w_mo"] = by_tiles(a["w_mo_2"])
    t["w_ff1"] = by_tiles(a["w_ff1_2"])
    t["w_ff2"] = by_tiles(a["w_ff2_2"])
    gates = np.zeros((DEPTH, P, 2, 4, P), np.float32)
    for n in range(8):
        r = slice(64 * (n % 2), 64 * (n % 2) + 64)
        for g, name in enumerate(("w_rg", "w_ig")):
            gates[:, r, g, n // 2, r] = a[name][:, n]
    t["w_gates"] = gates
    dist = REL_CLIP + np.arange(P)[:, None] - np.arange(256)[None, :]
    t["rel_bias"] = np.ascontiguousarray(a["rel_bias_2"][:, :, np.clip(dist, -(CHUNK - 1), REL_CLIP) + CHUNK - 1])
    pieces = [per_partition(a["norm_mix_g"])]
    pieces += [np.tile(a[n], (1, 2))[:, None, :] for n in ("q_norm_g", "k_norm_g")]
    pieces += [a["subln_g"][:, None, :]]
    pieces += [a["conv_w"].reshape(DEPTH, 4, 4, P).transpose(0, 2, 1, 3).reshape(DEPTH, 16, P)]
    pieces += [per_partition(a[n]) for n in ("conv_b", "b_rg", "b_ig", "lru_L", "rec_norm_g", "norm_ffn_g")]
    lam = np.concatenate([a[n] for n in ("lambda_q1", "lambda_k1", "lambda_q2", "lambda_k2")], axis=1)
    t["lambdas"] = np.ascontiguousarray(np.broadcast_to(lam.reshape(1, -1), (P, DEPTH * 4 * HEAD_DIM)))
    t["params1"] = np.ascontiguousarray(np.concatenate(pieces, axis=1).transpose(2, 0, 1))
    pieces = [a["conv_w_2"].reshape(DEPTH, 3, 2, P).transpose(0, 2, 1, 3).reshape(DEPTH, 6, P)]
    pieces += [per_partition(a[n]) for n in ("ln1_g_2", "ln1_b_2", "ln2_g_2", "ln2_b_2", "ln3_g_2", "ln3_b_2")]
    t["params2"] = np.ascontiguousarray(np.concatenate(pieces, axis=1).transpose(2, 0, 1))
    t["consts"] = constants()
    return t


def kernel(**inputs):
    import concourse.bacc as bacc
    from concourse.bass_utils import run_bass_kernel_spmd

    arrays = layout({name: np.asarray(a) for name, a in inputs.items()})
    nc = bacc.Bacc("TRN2", target_bir_lowering=False, num_devices=1)
    feed, aps = {}, {}
    for name, a in arrays.items():
        feed[f"in_{name}"] = a
        aps[name] = nc.dram_tensor(f"in_{name}", a.shape, mybir.dt.from_np(a.dtype), kind="ExternalInput").ap()
    out = nc.dram_tensor("out_x", (P, DC, SEQ), F32, kind="ExternalOutput").ap()
    build(nc, aps, out)
    r = run_bass_kernel_spmd(nc, [feed], core_ids=[0])
    x = r.results[0]["out_x"]
    return np.ascontiguousarray(x.transpose(1, 0, 2).reshape(D, SEQ).T)[None]
```
